# Optimizing a Trainium2 kernel written in Bass

```python
import math
import jax, jax.numpy as jnp
from jax import lax
import numpy as np

D_MODEL = 1024
BATCH = 1
SEQ = 256
DEPTH = 2

GRID_W = 64
CTX_LEN = 256
HEAD_DIM = 64
A_Q_HEADS = 8
A_KV_HEADS = 2
B_HEADS = 4
B_KEY_DIM = 128
B_VAL_DIM = 128
HGRN_CHUNK = 32
C_HEADS = 16
NA_ROWS = 8
NA_COLS = 16
D_FF = 2816
CONV_W = 3

ROPE_THETA = 10000.0
Q_BLOCK = 128
EPS = 1e-6
ATTN_SCALE = HEAD_DIM ** -0.5
HGRN_SCALE = B_KEY_DIM ** -0.5

N_EVEN = (DEPTH + 1) // 2
N_ODD = DEPTH // 2
A_Q_W = A_Q_HEADS * HEAD_DIM
A_KV_W = A_KV_HEADS * HEAD_DIM
B_K_W = B_HEADS * B_KEY_DIM
B_V_W = B_HEADS * B_VAL_DIM
EVEN_IN_W = A_Q_W + 2 * A_KV_W + 3 * B_K_W + 2 * B_V_W
EVEN_SPLITS = (A_Q_W, A_Q_W + A_KV_W, A_Q_W + 2 * A_KV_W, A_Q_W + 2 * A_KV_W + B_K_W,
               A_Q_W + 2 * A_KV_W + 2 * B_K_W, A_Q_W + 2 * A_KV_W + 3 * B_K_W,
               A_Q_W + 2 * A_KV_W + 3 * B_K_W + B_V_W)
EVEN_OUT_W = A_Q_W + B_V_W
C_W = C_HEADS * HEAD_DIM


def rms_norm(x, w):
    xf = x.astype(jnp.float32)
    y = xf * lax.rsqrt(jnp.mean(xf * xf, axis=-1, keepdims=True) + EPS)
    return (y * w.astype(jnp.float32)).astype(x.dtype)

def axial_rope_tables(n_tokens):
    t = jnp.arange(n_tokens)
    row = (t // GRID_W).astype(jnp.float32)
    col = (t % GRID_W).astype(jnp.float32)
    n_freq = HEAD_DIM // 4
    inv_freq = ROPE_THETA ** (-jnp.arange(n_freq, dtype=jnp.float32) / n_freq)
    ang = jnp.concatenate([row[:, None] * inv_freq, col[:, None] * inv_freq], axis=-1)
    return jnp.cos(ang), jnp.sin(ang)

def apply_rope(x, cos, sin):
    x1, x2 = jnp.split(x, 2, axis=-1)
    c = cos[None, :, None, :].astype(x.dtype)
    s = sin[None, :, None, :].astype(x.dtype)
    return jnp.concatenate([x1 * c - x2 * s, x1 * s + x2 * c], axis=-1)

def gqa_axial_attention(q_lat, k_lat, v_lat, q_ctx, k_ctx, v_ctx, q_norm_w, k_norm_w, with_ctx_out):
    B_, L = q_lat.shape[:2]
    n_ctx = q_ctx.shape[1]
    group = A_Q_HEADS // A_KV_HEADS
    q_lat, q_ctx = rms_norm(q_lat, q_norm_w), rms_norm(q_ctx, q_norm_w)
    k_lat, k_ctx = rms_norm(k_lat, k_norm_w), rms_norm(k_ctx, k_norm_w)
    cos, sin = axial_rope_tables(L)
    q_lat = apply_rope(q_lat, cos, sin)
    k_lat = apply_rope(k_lat, cos, sin)
    k_all = jnp.concatenate([k_ctx, k_lat], axis=1)
    v_all = jnp.concatenate([v_ctx, v_lat], axis=1)

    def attend(q, k, v):
        s = jnp.einsum("bqhgd,bkhd->bhgqk", q, k).astype(jnp.float32) * ATTN_SCALE
        p = jax.nn.softmax(s, axis=-1).astype(v.dtype)
        return jnp.einsum("bhgqk,bkhd->bqhgd", p, v)

    n_blk = L // Q_BLOCK
    q_blocks = q_lat.reshape(B_, n_blk, Q_BLOCK, A_KV_HEADS, group, HEAD_DIM).transpose(1, 0, 2, 3, 4, 5)
    o = lax.map(lambda qb: attend(qb, k_all, v_all), q_blocks)
    o_lat = o.transpose(1, 0, 2, 3, 4, 5).reshape(B_, L, A_Q_W)
    o_ctx = None
    if with_ctx_out:
        o_ctx = attend(q_ctx.reshape(B_, n_ctx, A_KV_HEADS, group, HEAD_DIM), k_ctx, v_ctx).reshape(B_, n_ctx, A_Q_W)
    return o_lat, o_ctx

def forget_gate(f_raw, lb):
    z = f_raw.astype(jnp.float32)
    log_f = jnp.logaddexp(jnp.log(lb), jnp.log1p(-lb) + jax.nn.log_sigmoid(z))
    k = (1.0 - lb) * jax.nn.sigmoid(-z)
    return k, log_f

def hgrn2_chunk_scan(q, k, log_f, v, s0):
    B_, L, H, dk = q.shape
    dv = v.shape[-1]
    n = L // HGRN_CHUNK

    def to_chunks(a):
        return a.reshape(B_, n, HGRN_CHUNK, H, a.shape[-1]).transpose(1, 0, 3, 2, 4)

    tri = jnp.tril(jnp.ones((HGRN_CHUNK, HGRN_CHUNK), dtype=bool))[None, None, :, :, None]

    def step(S, inp):
        qc, kc, gc, vc = inp
        b = jnp.cumsum(gc, axis=2)
        diff = b[:, :, :, None, :] - b[:, :, None, :, :]
        decay = jnp.exp(jnp.where(tri, diff, -jnp.inf))
        scores = jnp.einsum("bhtd,bhtsd,bhsd->bhts", qc, decay, kc)
        o = jnp.einsum("bhts,bhsv->bhtv", scores, vc) + jnp.einsum("bhtd,bhdv->bhtv", qc * jnp.exp(b), S)
        b_last = b[:, :, -1:, :]
        S_new = jnp.exp(b_last[:, :, 0, :])[..., None] * S + jnp.einsum("bhsd,bhsv->bhdv", kc * jnp.exp(b_last - b), vc)
        return S_new, o

    S, o = lax.scan(step, s0, (to_chunks(q), to_chunks(k), to_chunks(log_f), to_chunks(v)))
    o = o.transpose(1, 0, 3, 2, 4).reshape(B_, L, H, dv).astype(v.dtype)
    return o, S

def hgrn2_bidirectional(q_lat, f_lat, i_lat, q_ctx, f_ctx, i_ctx, lb):
    B_ = q_lat.shape[0]
    s0 = jnp.zeros((B_, B_HEADS, B_KEY_DIM, B_VAL_DIM), jnp.float32)
    o_lat, o_ctx = None, None
    for d in range(2):
        flip = (lambda a: a) if d == 0 else (lambda a: a[:, ::-1])
        k_l, lf_l = forget_gate(f_lat[d], lb[d])
        k_c, lf_c = forget_gate(f_ctx[d], lb[d])
        oc, s_ctx = hgrn2_chunk_scan(flip(q_ctx), flip(k_c), flip(lf_c), flip(i_ctx), s0)
        ol, _ = hgrn2_chunk_scan(flip(q_lat), flip(k_l), flip(lf_l), flip(i_lat), s_ctx)
        o_lat = flip(ol) if o_lat is None else o_lat + flip(ol)
        o_ctx = flip(oc) if o_ctx is None else o_ctx + flip(oc)
    return o_lat, o_ctx

def even_mixer(h_lat, h_ctx, w_in, w_out, q_norm_w, k_norm_w, lb, out_norm_w, with_ctx_out):
    def project(h):
        B_, n = h.shape[:2]
        aq, ak, av, bq, bff, bfb, bi, bg = jnp.split(h @ w_in, EVEN_SPLITS, axis=-1)
        bshape = (B_, n, B_HEADS, B_KEY_DIM)
        return (aq.reshape(B_, n, A_Q_HEADS, HEAD_DIM), ak.reshape(B_, n, A_KV_HEADS, HEAD_DIM),
                av.reshape(B_, n, A_KV_HEADS, HEAD_DIM), (jax.nn.silu(bq) * HGRN_SCALE).reshape(bshape),
                (bff.reshape(bshape), bfb.reshape(bshape)), bi.reshape(B_, n, B_HEADS, B_VAL_DIM), bg)

    aq_l, ak_l, av_l, bq_l, bf_l, bi_l, bg_l = project(h_lat)
    aq_c, ak_c, av_c, bq_c, bf_c, bi_c, bg_c = project(h_ctx)
    oa_lat, oa_ctx = gqa_axial_attention(aq_l, ak_l, av_l, aq_c, ak_c, av_c, q_norm_w, k_norm_w, with_ctx_out)
    ob_lat, ob_ctx = hgrn2_bidirectional(bq_l, bf_l, bi_l, bq_c, bf_c, bi_c, lb)

    def readout(o, g):
        B_, n = o.shape[:2]
        return (rms_norm(o, out_norm_w).reshape(B_, n, B_V_W) * jax.nn.silu(g)).astype(g.dtype)

    y_lat = jnp.concatenate([oa_lat, readout(ob_lat, bg_l)], axis=-1) @ w_out
    y_ctx = None
    if with_ctx_out:
        y_ctx = jnp.concatenate([oa_ctx, readout(ob_ctx, bg_c)], axis=-1) @ w_out
    return y_lat, y_ctx

def odd_mixer(h_lat, h_ctx, w_qkv, w_out, rpb, with_ctx_out):
    B_, L, _ = h_lat.shape
    n_ctx = h_ctx.shape[1]
    rows = L // GRID_W
    wr = min(NA_ROWS, rows)
    qkv = (h_lat @ w_qkv).reshape(B_, rows, GRID_W, 3, C_HEADS, HEAD_DIM)
    q, k, v = qkv[:, :, :, 0], qkv[:, :, :, 1], qkv[:, :, :, 2]
    qkv_c = (h_ctx @ w_qkv).reshape(B_, n_ctx, 3, C_HEADS, HEAD_DIM)
    q_c, k_c, v_c = qkv_c[:, :, 0], qkv_c[:, :, 1], qkv_c[:, :, 2]

    r_start = jnp.clip(jnp.arange(rows) - wr // 2, 0, rows - wr)
    c_start = jnp.clip(jnp.arange(GRID_W) - NA_COLS // 2, 0, GRID_W - NA_COLS)
    c_idx = c_start[:, None] + jnp.arange(NA_COLS)
    dx = c_idx - jnp.arange(GRID_W)[:, None] + (NA_COLS - 1)

    def row_block(inp):
        r, q_r = inp
        r0 = r_start[r]
        k_band = lax.dynamic_slice_in_dim(k, r0, wr, axis=1)
        v_band = lax.dynamic_slice_in_dim(v, r0, wr, axis=1)
        k_win = k_band[:, :, c_idx]
        v_win = v_band[:, :, c_idx]
        dy = r0 + jnp.arange(wr) - r + (NA_ROWS - 1)
        bias = rpb[:, dy[:, None, None], dx[None, :, :]].transpose(0, 2, 1, 3)
        s_loc = jnp.einsum("bqhd,brqjhd->bhqrj", q_r, k_win).astype(jnp.float32) * ATTN_SCALE
        s_loc = (s_loc + bias[None].astype(jnp.float32)).reshape(B_, C_HEADS, GRID_W, wr * NA_COLS)
        s_ctx = jnp.einsum("bqhd,bchd->bhqc", q_r, k_c).astype(jnp.float32) * ATTN_SCALE
        p = jax.nn.softmax(jnp.concatenate([s_loc, s_ctx], axis=-1), axis=-1).astype(v.dtype)
        p_loc = p[..., :wr * NA_COLS].reshape(B_, C_HEADS, GRID_W, wr, NA_COLS)
        p_ctx = p[..., wr * NA_COLS:]
        return jnp.einsum("bhqrj,brqjhd->bqhd", p_loc, v_win) + jnp.einsum("bhqc,bchd->bqhd", p_ctx, v_c)

    o = lax.map(row_block, (jnp.arange(rows), q.transpose(1, 0, 2, 3, 4)))
    y_lat = o.transpose(1, 0, 2, 3, 4).reshape(B_, L, C_W) @ w_out
    y_ctx = None
    if with_ctx_out:
        s = jnp.einsum("bqhd,bkhd->bhqk", q_c, k_c).astype(jnp.float32) * ATTN_SCALE
        p = jax.nn.softmax(s, axis=-1).astype(v_c.dtype)
        y_ctx = jnp.einsum("bhqk,bkhd->bqhd", p, v_c).reshape(B_, n_ctx, C_W) @ w_out
    return y_lat, y_ctx

def conv_ffn(h, w_up, conv_w, conv_b, w_down):
    u = h @ w_up
    u = lax.conv_general_dilated(u, conv_w[:, None, :], window_strides=(1,),
                                 padding=[(CONV_W // 2, CONV_W // 2)],
                                 dimension_numbers=("NWC", "WIO", "NWC"),
                                 feature_group_count=u.shape[-1]) + conv_b
    a, g = jnp.split(u, 2, axis=-1)
    return (jax.nn.silu(g) * a) @ w_down

def first_inputs(seed: int = 0) -> dict:
    key = jax.random.key(seed)
    ks = jax.random.split(key, 24)

    def nrm(k, shape, s):
        return jax.random.normal(k, shape, jnp.float32) * s

    return {
        "x": nrm(ks[0], (BATCH, SEQ, D_MODEL), 1.0),
        "c": nrm(ks[1], (BATCH, D_MODEL), 1.0),
        "ctx": nrm(ks[2], (BATCH, CTX_LEN, D_MODEL), 1.0),
        "c_ctx": nrm(ks[3], (D_MODEL,), 1.0),
        "w_mod": nrm(ks[4], (DEPTH, D_MODEL, 6 * D_MODEL), D_MODEL ** -0.5),
        "b_mod": nrm(ks[5], (DEPTH, 6 * D_MODEL), 0.02),
        "norm_pre_mix": 1.0 + nrm(ks[6], (DEPTH, D_MODEL), 0.1),
        "norm_post_mix": 1.0 + nrm(ks[7], (DEPTH, D_MODEL), 0.1),
        "norm_pre_ffn": 1.0 + nrm(ks[8], (DEPTH, D_MODEL), 0.1),
        "norm_post_ffn": 1.0 + nrm(ks[9], (DEPTH, D_MODEL), 0.1),
        "even_w_in": nrm(ks[10], (N_EVEN, D_MODEL, EVEN_IN_W), D_MODEL ** -0.5),
        "even_w_out": nrm(ks[11], (N_EVEN, EVEN_OUT_W, D_MODEL), EVEN_OUT_W ** -0.5),
        "even_q_norm": 1.0 + nrm(ks[12], (N_EVEN, HEAD_DIM), 0.1),
        "even_k_norm": 1.0 + nrm(ks[13], (N_EVEN, HEAD_DIM), 0.1),
        "hgrn_lb_logits": nrm(ks[14], (N_EVEN, 2, B_K_W), 1.0),
        "hgrn_out_norm": 1.0 + nrm(ks[15], (N_EVEN, B_VAL_DIM), 0.1),
        "odd_w_qkv": nrm(ks[16], (N_ODD, D_MODEL, 3 * C_W), D_MODEL ** -0.5),
        "odd_w_out": nrm(ks[17], (N_ODD, C_W, D_MODEL), C_W ** -0.5),
        "odd_rpb": nrm(ks[18], (N_ODD, C_HEADS, 2 * NA_ROWS - 1, 2 * NA_COLS - 1), 0.1),
        "ffn_w_up": nrm(ks[19], (DEPTH, D_MODEL, 2 * D_FF), D_MODEL ** -0.5),
        "ffn_conv_w": nrm(ks[20], (DEPTH, CONV_W, 2 * D_FF), CONV_W ** -0.5),
        "ffn_conv_b": nrm(ks[21], (DEPTH, 2 * D_FF), 0.02),
        "ffn_w_down": nrm(ks[22], (DEPTH, D_FF, D_MODEL), D_FF ** -0.5),
    }

def first_block(x, c, ctx, c_ctx, w_mod, b_mod, norm_pre_mix, norm_post_mix, norm_pre_ffn, norm_post_ffn,
              even_w_in, even_w_out, even_q_norm, even_k_norm, hgrn_lb_logits, hgrn_out_norm,
              odd_w_qkv, odd_w_out, odd_rpb, ffn_w_up, ffn_conv_w, ffn_conv_b, ffn_w_down):
    p_lb = jax.nn.softmax(hgrn_lb_logits.astype(jnp.float32), axis=0)
    lb_all = jnp.concatenate([jnp.zeros_like(p_lb[:1]), jnp.cumsum(p_lb[1:], axis=0)], axis=0)
    lb_all = lb_all.reshape(N_EVEN, 2, B_HEADS, B_KEY_DIM)

    for l in range(DEPTH):
        with_ctx_out = l < DEPTH - 1
        mod_lat = (jax.nn.silu(c) @ w_mod[l] + b_mod[l])[:, None, :]
        mod_ctx = (jax.nn.silu(c_ctx) @ w_mod[l] + b_mod[l])[None, None, :]
        sh1, sc1, g1, sh2, sc2, g2 = jnp.split(mod_lat, 6, axis=-1)
        sh1c, sc1c, g1c, sh2c, sc2c, g2c = jnp.split(mod_ctx, 6, axis=-1)

        h_lat = rms_norm(x, norm_pre_mix[l]) * (1.0 + sc1) + sh1
        h_ctx = rms_norm(ctx, norm_pre_mix[l]) * (1.0 + sc1c) + sh1c
        if l % 2 == 0:
            e = l // 2
            y_lat, y_ctx = even_mixer(h_lat, h_ctx, even_w_in[e], even_w_out[e], even_q_norm[e], even_k_norm[e],
                                      lb_all[e], hgrn_out_norm[e], with_ctx_out)
        else:
            o = l // 2
            y_lat, y_ctx = odd_mixer(h_lat, h_ctx, odd_w_qkv[o], odd_w_out[o], odd_rpb[o], with_ctx_out)
        x = x + g1 * rms_norm(y_lat, norm_post_mix[l])

        h_lat = rms_norm(x, norm_pre_ffn[l]) * (1.0 + sc2) + sh2
        x = x + g2 * rms_norm(conv_ffn(h_lat, ffn_w_up[l], ffn_conv_w[l], ffn_conv_b[l], ffn_w_down[l]), norm_post_ffn[l])
        if with_ctx_out:
            ctx = ctx + g1c * rms_norm(y_ctx, norm_post_mix[l])
            h_ctx = rms_norm(ctx, norm_pre_ffn[l]) * (1.0 + sc2c) + sh2c
            ctx = ctx + g2c * rms_norm(conv_ffn(h_ctx, ffn_w_up[l], ffn_conv_w[l], ffn_conv_b[l], ffn_w_down[l]), norm_post_ffn[l])
    return x


CHUNK = 64
N_BRANCH = 3
POOL_GROUPS = 4
POOL_GW = 128
POOL_W = POOL_GROUPS * POOL_GW
POOL_WINDOWS = (2, 4, 8, 16)
ML_HEADS = 4
ML_DH = 128
ML_W = ML_HEADS * ML_DH
CONV_W_2 = 4
FOX_HEADS = 8
FOX_DH = 64
FOX_W = FOX_HEADS * FOX_DH
N_EXPERTS = 8
TOP_K = 2
D_FF_EXPERT = 3584
MOE_BLOCK = 128
NORM_EPS = 1e-6
IN_SIZES = (POOL_W, ML_W, ML_W, ML_W, ML_W, ML_HEADS, ML_HEADS, FOX_W, FOX_W, FOX_W, FOX_HEADS, N_BRANCH * D_MODEL)
IN_W = sum(IN_SIZES)
N_DENSE = (DEPTH + 1) // 2
N_MOE = DEPTH // 2


def rmsnorm(x, g):
    xf = x.astype(jnp.float32)
    y = xf * lax.rsqrt(jnp.mean(xf * xf, axis=-1, keepdims=True) + NORM_EPS)
    return (y * g.astype(jnp.float32)).astype(x.dtype)

def causal_depthwise_conv(u, w):
    return lax.conv_general_dilated(u, w[:, None, :].astype(u.dtype), window_strides=(1,),
                                    padding=[(CONV_W_2 - 1, 0)], dimension_numbers=('NWC', 'WIO', 'NWC'),
                                    feature_group_count=u.shape[-1])

def pool_mixer(u, w_grp, scale):
    bsz, s_len, _ = u.shape
    uf = u.astype(jnp.float32).reshape(bsz, s_len, POOL_GROUPS, POOL_GW)
    cs = jnp.concatenate([jnp.zeros_like(uf[:, :1]), jnp.cumsum(uf, axis=1)], axis=1)
    pos = jnp.arange(s_len)
    outs = []
    for g, w in enumerate(POOL_WINDOWS):
        csg = cs[:, :, g]
        lower = jnp.concatenate([jnp.zeros_like(csg[:, :w - 1]), csg[:, :s_len - w + 1]], axis=1)
        cnt = jnp.minimum(pos + 1, w).astype(jnp.float32)[None, :, None]
        outs.append((csg[:, 1:] - lower) / cnt - uf[:, :, g])
    d = jnp.stack(outs, axis=2)
    y = jnp.einsum('bsgc,gcd->bsgd', d, w_grp.astype(jnp.float32)).reshape(bsz, s_len, POOL_W)
    return (y * scale.astype(jnp.float32)).astype(u.dtype)

def mlstm_mixer(q, k, v, o_pre, i_pre, f_pre, g_norm):
    bsz, s_len, _ = q.shape
    nc = s_len // CHUNK

    def heads(t):
        return t.astype(jnp.float32).reshape(bsz, nc, CHUNK, ML_HEADS, ML_DH).transpose(1, 0, 3, 2, 4)

    def gates(t):
        return t.astype(jnp.float32).reshape(bsz, nc, CHUNK, ML_HEADS).transpose(1, 0, 3, 2)

    qc, kc, vc = heads(q), heads(k) * (ML_DH ** -0.5), heads(v)
    lic = gates(i_pre)
    lfc = gates(jax.nn.log_sigmoid(f_pre.astype(jnp.float32)))
    tri = jnp.tril(jnp.ones((CHUNK, CHUNK), dtype=bool))

    def step(carry, inp):
        c_mat, n_vec, m = carry
        qb, kb, vb, li, lf = inp
        b = jnp.cumsum(lf, axis=-1)
        dmat = jnp.where(tri, b[..., :, None] - b[..., None, :] + li[..., None, :], -jnp.inf)
        m_inter = b + m[..., None]
        m_t = jnp.maximum(m_inter, jnp.max(dmat, axis=-1))
        w_inter = jnp.exp(m_inter - m_t)
        p = jnp.exp(dmat - m_t[..., None]) * jnp.einsum('bhtd,bhsd->bhts', qb, kb)
        num = w_inter[..., None] * jnp.einsum('bhvk,bhtk->bhtv', c_mat, qb) + jnp.einsum('bhts,bhsv->bhtv', p, vb)
        den = w_inter * jnp.einsum('bhk,bhtk->bht', n_vec, qb) + jnp.sum(p, axis=-1)
        h = num / jnp.maximum(jnp.abs(den), jnp.exp(-m_t))[..., None]
        b_last = b[..., -1]
        g = b_last[..., None] - b + li
        m_new = jnp.maximum(b_last + m, jnp.max(g, axis=-1))
        decay = jnp.exp(b_last + m - m_new)
        wk = jnp.exp(g - m_new[..., None])
        c_mat = decay[..., None, None] * c_mat + jnp.einsum('bhs,bhsv,bhsk->bhvk', wk, vb, kb)
        n_vec = decay[..., None] * n_vec + jnp.einsum('bhs,bhsk->bhk', wk, kb)
        return (c_mat, n_vec, m_new), h

    init = (jnp.zeros((bsz, ML_HEADS, ML_DH, ML_DH), jnp.float32),
            jnp.zeros((bsz, ML_HEADS, ML_DH), jnp.float32),
            jnp.zeros((bsz, ML_HEADS), jnp.float32))
    _, h = lax.scan(step, init, (qc, kc, vc, lic, lfc))
    h = h.transpose(1, 0, 3, 2, 4)
    h = h * lax.rsqrt(jnp.mean(h * h, axis=-1, keepdims=True) + NORM_EPS) * g_norm.astype(jnp.float32).reshape(ML_HEADS, ML_DH)
    h = h.reshape(bsz, s_len, ML_W) * jax.nn.sigmoid(o_pre.astype(jnp.float32))
    return h.astype(q.dtype)

def fox_mixer(q, k, v, f_pre):
    bsz, s_len, _ = q.shape
    nb = s_len // Q_BLOCK
    qh = q.reshape(bsz, s_len, FOX_HEADS, FOX_DH).transpose(0, 2, 1, 3)
    kh = k.reshape(bsz, s_len, FOX_HEADS, FOX_DH).transpose(0, 2, 1, 3)
    vh = v.reshape(bsz, s_len, FOX_HEADS, FOX_DH).transpose(0, 2, 1, 3)
    f_cum = jnp.cumsum(jax.nn.log_sigmoid(f_pre.astype(jnp.float32)), axis=1).transpose(0, 2, 1)
    q_blocks = qh.reshape(bsz, FOX_HEADS, nb, Q_BLOCK, FOX_DH).transpose(2, 0, 1, 3, 4)
    f_blocks = f_cum.reshape(bsz, FOX_HEADS, nb, Q_BLOCK).transpose(2, 0, 1, 3)
    kpos = jnp.arange(s_len)
    scale = FOX_DH ** -0.5

    def block(args):
        qb, fq, i = args
        qpos = i * Q_BLOCK + jnp.arange(Q_BLOCK)
        s = jnp.einsum('bhtd,bhsd->bhts', qb, kh).astype(jnp.float32) * scale + fq[..., :, None] - f_cum[:, :, None, :]
        s = jnp.where(kpos[None, :] <= qpos[:, None], s, -jnp.inf)
        p = jax.nn.softmax(s, axis=-1)
        return jnp.einsum('bhts,bhsd->bhtd', p.astype(vh.dtype), vh)

    o = lax.map(block, (q_blocks, f_blocks, jnp.arange(nb)))
    return o.transpose(1, 0, 3, 2, 4).reshape(bsz, s_len, FOX_W)

def token_mixing(x, norm_g, w_in, pool_w_grp, pool_scale, ml_conv_w, ml_b_i, ml_b_f, ml_norm_g,
                 fox_b_f, w_br_pool, w_br_ml, w_br_fox, w_out):
    h = rmsnorm(x, norm_g)
    proj = h @ w_in
    splits = np.cumsum(IN_SIZES)[:-1].tolist()
    (u_pool, ml_q, ml_k, ml_v, ml_o, ml_i, ml_f, fx_q, fx_k, fx_v, fx_f, gate_pre) = jnp.split(proj, splits, axis=-1)
    qk = jax.nn.silu(causal_depthwise_conv(jnp.concatenate([ml_q, ml_k], axis=-1), ml_conv_w))
    ml_q, ml_k = qk[..., :ML_W], qk[..., ML_W:]
    y_pool = pool_mixer(u_pool, pool_w_grp, pool_scale) @ w_br_pool
    y_ml = mlstm_mixer(ml_q, ml_k, ml_v, ml_o, ml_i + ml_b_i, ml_f + ml_b_f, ml_norm_g) @ w_br_ml
    y_fox = fox_mixer(fx_q, fx_k, fx_v, fx_f + fox_b_f) @ w_br_fox
    gts = jax.nn.sigmoid(gate_pre).reshape(gate_pre.shape[:-1] + (N_BRANCH, D_MODEL))
    merged = gts[..., 0, :] * y_pool + gts[..., 1, :] * y_ml + gts[..., 2, :] * y_fox
    return merged @ w_out

def swiglu(h, w_gate, w_up, w_down):
    return (jax.nn.silu(h @ w_gate) * (h @ w_up)) @ w_down

def moe_swiglu(h, w_router, b_router, w_gate, w_up, w_down):
    bsz, s_len, d = h.shape
    n_tok = bsz * s_len
    t = h.reshape(n_tok, d)
    logits = (t @ w_router).astype(jnp.float32) + b_router.astype(jnp.float32)
    top_v, top_e = lax.top_k(logits, TOP_K)
    gate = jax.nn.softmax(top_v, axis=-1)
    n_asg = n_tok * TOP_K
    e_flat = top_e.reshape(n_asg)
    tok_flat = jnp.repeat(jnp.arange(n_tok, dtype=jnp.int32), TOP_K)
    g_flat = gate.reshape(n_asg)
    order = jnp.argsort(e_flat)
    e_s, tok_s, g_s = e_flat[order], tok_flat[order], g_flat[order]
    counts = jnp.bincount(e_flat, length=N_EXPERTS).astype(jnp.int32)
    start = jnp.cumsum(counts) - counts
    padded = ((counts + MOE_BLOCK - 1) // MOE_BLOCK) * MOE_BLOCK
    pend = jnp.cumsum(padded)
    pstart = pend - padded
    dest = pstart[e_s] + (jnp.arange(n_asg, dtype=jnp.int32) - start[e_s])
    n_blk = (n_asg + N_EXPERTS * (MOE_BLOCK - 1) + MOE_BLOCK - 1) // MOE_BLOCK
    n_rows = n_blk * MOE_BLOCK
    row_tok = jnp.full((n_rows,), n_tok, dtype=jnp.int32).at[dest].set(tok_s)
    row_g = jnp.zeros((n_rows,), jnp.float32).at[dest].set(g_s)
    blk_e = jnp.minimum(jnp.searchsorted(pend, jnp.arange(n_blk, dtype=jnp.int32) * MOE_BLOCK, side='right'), N_EXPERTS - 1)
    t_pad = jnp.concatenate([t, jnp.zeros((1, d), t.dtype)], axis=0)
    xr = t_pad[row_tok].reshape(n_blk, MOE_BLOCK, d)

    def one(args):
        xb, e = args
        return (jax.nn.silu(xb @ w_gate[e]) * (xb @ w_up[e])) @ w_down[e]

    out = lax.map(one, (xr, blk_e)).reshape(n_rows, d)
    y = jnp.zeros((n_tok + 1, d), out.dtype).at[row_tok].add(out * row_g[:, None].astype(out.dtype))[:n_tok]
    return y.reshape(bsz, s_len, d)

def second_inputs(seed: int = 0) -> dict:
    key = jax.random.key(seed)
    ks = iter(jax.random.split(key, 32))

    def nrm(shape, scale):
        return jax.random.normal(next(ks), shape, jnp.float32) * scale

    return {
        'x': nrm((BATCH, SEQ, D_MODEL), 1.0),
        'mix_norm_g': 1.0 + nrm((DEPTH, D_MODEL), 0.05),
        'w_in': nrm((DEPTH, D_MODEL, IN_W), D_MODEL ** -0.5),
        'pool_w_grp': nrm((DEPTH, POOL_GROUPS, POOL_GW, POOL_GW), POOL_GW ** -0.5),
        'pool_scale': 1.0 + nrm((DEPTH, POOL_W), 0.05),
        'ml_conv_w': nrm((DEPTH, CONV_W_2, 2 * ML_W), CONV_W_2 ** -0.5),
        'ml_b_i': nrm((DEPTH, ML_HEADS), 0.1),
        'ml_b_f': 3.0 + nrm((DEPTH, ML_HEADS), 0.5),
        'ml_norm_g': 1.0 + nrm((DEPTH, ML_W), 0.05),
        'fox_b_f': 3.0 + nrm((DEPTH, FOX_HEADS), 0.5),
        'w_br_pool': nrm((DEPTH, POOL_W, D_MODEL), POOL_W ** -0.5),
        'w_br_ml': nrm((DEPTH, ML_W, D_MODEL), ML_W ** -0.5),
        'w_br_fox': nrm((DEPTH, FOX_W, D_MODEL), FOX_W ** -0.5),
        'w_out': nrm((DEPTH, D_MODEL, D_MODEL), D_MODEL ** -0.5),
        'ffn_norm_g': 1.0 + nrm((DEPTH, D_MODEL), 0.05),
        'ff_w_gate': nrm((N_DENSE, D_MODEL, D_FF), D_MODEL ** -0.5),
        'ff_w_up': nrm((N_DENSE, D_MODEL, D_FF), D_MODEL ** -0.5),
        'ff_w_down': nrm((N_DENSE, D_FF, D_MODEL), D_FF ** -0.5),
        'moe_w_router': nrm((N_MOE, D_MODEL, N_EXPERTS), D_MODEL ** -0.5),
        'moe_b_router': nrm((N_MOE, N_EXPERTS), 0.01),
        'moe_w_gate': nrm((N_MOE, N_EXPERTS, D_MODEL, D_FF_EXPERT), D_MODEL ** -0.5),
        'moe_w_up': nrm((N_MOE, N_EXPERTS, D_MODEL, D_FF_EXPERT), D_MODEL ** -0.5),
        'moe_w_down': nrm((N_MOE, N_EXPERTS, D_FF_EXPERT, D_MODEL), D_FF_EXPERT ** -0.5),
        'final_norm_g': 1.0 + nrm((D_MODEL,), 0.05),
    }

def second_block(x, mix_norm_g, w_in, pool_w_grp, pool_scale, ml_conv_w, ml_b_i, ml_b_f, ml_norm_g, fox_b_f,
              w_br_pool, w_br_ml, w_br_fox, w_out, ffn_norm_g, ff_w_gate, ff_w_up, ff_w_down,
              moe_w_router, moe_b_router, moe_w_gate, moe_w_up, moe_w_down, final_norm_g):
    for l in range(DEPTH):
        x = x + token_mixing(x, mix_norm_g[l], w_in[l], pool_w_grp[l], pool_scale[l], ml_conv_w[l],
                             ml_b_i[l], ml_b_f[l], ml_norm_g[l], fox_b_f[l], w_br_pool[l], w_br_ml[l],
                             w_br_fox[l], w_out[l])
        h = rmsnorm(x, ffn_norm_g[l])
        if l % 2 == 0:
            x = x + swiglu(h, ff_w_gate[l // 2], ff_w_up[l // 2], ff_w_down[l // 2])
        else:
            x = x + moe_swiglu(h, moe_w_router[l // 2], moe_b_router[l // 2], moe_w_gate[l // 2],
                               moe_w_up[l // 2], moe_w_down[l // 2])
    return rmsnorm(x, final_norm_g)


def setup_inputs(seed=0):
    out = dict(first_inputs(seed))
    for name, value in second_inputs(seed + 1).items():
        if name != "x":
            out[name + "_2"] = value
    return out


def reference(
    x, c, ctx, c_ctx, w_mod, b_mod, norm_pre_mix, norm_post_mix, norm_pre_ffn, norm_post_ffn,
    even_w_in, even_w_out, even_q_norm, even_k_norm, hgrn_lb_logits, hgrn_out_norm, odd_w_qkv,
    odd_w_out, odd_rpb, ffn_w_up, ffn_conv_w, ffn_conv_b, ffn_w_down, mix_norm_g_2, w_in_2,
    pool_w_grp_2, pool_scale_2, ml_conv_w_2, ml_b_i_2, ml_b_f_2, ml_norm_g_2, fox_b_f_2,
    w_br_pool_2, w_br_ml_2, w_br_fox_2, w_out_2, ffn_norm_g_2, ff_w_gate_2, ff_w_up_2,
    ff_w_down_2, moe_w_router_2, moe_b_router_2, moe_w_gate_2, moe_w_up_2, moe_w_down_2,
    final_norm_g_2,
):
    x = first_block(
        x, c, ctx, c_ctx, w_mod, b_mod, norm_pre_mix, norm_post_mix, norm_pre_ffn,
        norm_post_ffn, even_w_in, even_w_out, even_q_norm, even_k_norm, hgrn_lb_logits,
        hgrn_out_norm, odd_w_qkv, odd_w_out, odd_rpb, ffn_w_up, ffn_conv_w, ffn_conv_b,
        ffn_w_down,
    )
    return second_block(
        x, mix_norm_g_2, w_in_2, pool_w_grp_2, pool_scale_2, ml_conv_w_2, ml_b_i_2, ml_b_f_2,
        ml_norm_g_2, fox_b_f_2, w_br_pool_2, w_br_ml_2, w_br_fox_2, w_out_2, ffn_norm_g_2,
        ff_w_gate_2, ff_w_up_2, ff_w_down_2, moe_w_router_2, moe_b_router_2, moe_w_gate_2,
        moe_w_up_2, moe_w_down_2, final_norm_g_2,
    )


_drawn_inputs = setup_inputs


def setup_inputs(seed=0):
    import zlib

    import numpy as np

    out = dict(_drawn_inputs(seed))
    spreads = {}
    factors = {'even_q_norm': 3.875,
     'even_k_norm': 3.469,
     'odd_rpb': 4.942,
     'ml_b_i_2': 64.0,
     'moe_b_router_2': 6.178,
     'ml_norm_g_2': 3.133}
    for name, (base, spread) in spreads.items():
        noise = np.random.default_rng([zlib.crc32(name.encode()), seed]).standard_normal(out[name].shape)
        drawn = base * np.exp(spread * noise) if base else spread * noise
        out[name] = __import__('jax').numpy.asarray(drawn.astype(out[name].dtype))
    for name, factor in factors.items():
        out[name] = (out[name] * factor).astype(out[name].dtype)
    return out
```

```python
import numpy as np
import concourse.bass as bass
from concourse import mybir
from contextlib import ExitStack

P = 128
D, T, TC = 1024, 256, 512
KT = D // P
DEPTH = 2
A_HEADS, A_KV, DH = 8, 2, 64
B_HEADS, DK = 4, 128
C_HEADS = 16
GRID_W, NA_ROWS, NA_COLS = 64, 8, 16
D_FF, FT = 2816, 2816 // P
POOL_WINDOWS = (2, 4, 8, 16)
ML_HEADS, FOX_HEADS = 4, 8
N_EXPERTS, D_FE = 8, 3584
ET = D_FE // P
EPS = 1e-6
NEG = -1e30
CAP = 96
NSLOT, SLOT = 4, 2048
DOWN_W, EDOWN_W = FT // 2 * P, ET // 2 * P
LEVELS = (0, 1, 2, 4, 8, 16, 32, 64)

STAGES = []
for _l in range(DEPTH):
    STAGES += [(f"mod{_l}", 24, SLOT), (f"proj{_l}", 14 if _l == 0 else 12, SLOT), (f"wout{_l}", 4, SLOT),
               (f"up{_l}", FT, SLOT), (f"down{_l}", 16, DOWN_W)]
for _l in range(DEPTH):
    STAGES += [(f"tproj{_l}", 16, SLOT), (f"gates{_l}", 12, SLOT), (f"branch{_l}", 8, 12 * P), (f"twout{_l}", 4, SLOT)]
    if _l == 0:
        STAGES += [("swup", FT, SLOT), ("swdown", 16, DOWN_W)]
STAGES += [("moe_up", N_EXPERTS * ET, SLOT), ("moe_down", N_EXPERTS * 16, EDOWN_W)]


def columns(parts):
    at, out = 0, {}
    for name, width in parts:
        out[name] = at
        at += width
    out["_end"] = at
    return out


CONSTS = columns([("ident", P), ("mean_d", P), ("mean_dk", P), ("mean_dh", P), ("ones", P), ("swap", P),
                  ("cos", T), ("sin", T), ("reset", TC), ("causal_add", P), ("causal_mul", P), ("nsel", 12),
                  ("rcount", 4 * T), ("ones_row", T), ("iota", CAP), ("eps", 1)])
PARAMS = columns([("c", KT * 2)] + [(f"b_mod{l}", 48) for l in range(DEPTH)]
                 + [(f"n{i}_{l}", KT) for l in range(DEPTH) for i in range(4)]
                 + [("q_norm", 1), ("k_norm", 1), ("out_norm", 1)]
                 + [(f"conv{l}", 2 * FT * 4) for l in range(DEPTH)]
                 + [(f"mix_g{l}", KT) for l in range(DEPTH)] + [(f"ffn_g{l}", KT) for l in range(DEPTH)]
                 + [(f"pool_scale{l}", 4) for l in range(DEPTH)] + [(f"ml_conv{l}", 8 * 4) for l in range(DEPTH)]
                 + [(f"ml_g{l}", 4) for l in range(DEPTH)] + [(f"b_i{l}", 1) for l in range(DEPTH)]
                 + [(f"b_f{l}", 1) for l in range(DEPTH)] + [(f"w_small{l}", KT * 16) for l in range(DEPTH)]
                 + [(f"w_grp{l}", 4 * P) for l in range(DEPTH)] + [("w_router", KT * N_EXPERTS), ("b_router", N_EXPERTS),
                 ("final_g", KT)])


def build(nc, dram, out):
    f32, u8, u32 = mybir.dt.float32, mybir.dt.uint8, mybir.dt.uint32
    ALU, ACT, AX = mybir.AluOpType, mybir.ActivationFunctionType, mybir.AxisListType

    base = {}
    units = {}
    at = 0
    for name, n, _ in STAGES:
        base[name], units[name] = at, n
        at += n
    MOE0 = base["moe_up"]
    PER_E = ET + 16

    ctx = ExitStack()
    with ctx:
        def sb(name, shape, dt=f32):
            return ctx.enter_context(nc.sbuf_tensor(name, shape, dt))

        sems = {}

        def S(name):
            if name not in sems:
                sems[name] = ctx.enter_context(nc.semaphore(name))
            return sems[name]

        ring = sb("ring", [P, NSLOT, SLOT])
        X = sb("X", [P, KT, TC])
        H = sb("H", [P, KT, TC])
        Y = sb("Y", [P, KT, TC])
        MIX = sb("MIX", [P, KT, TC])
        PROJ = sb("PROJ", [P, 12288])
        VT = sb("VT", [P, 2560])
        SC = sb("SC", [P, 2048])
        PR = sb("PR", [P, 2, TC])
        PTB = sb("PTB", [P, 2, TC])
        RT = sb("RT", [P, TC])
        cst = sb("cst", [P, CONSTS["_end"]])
        par = sb("par", [P, PARAMS["_end"]])
        lmask = sb("lmask", [P, 2 * len(LEVELS) * P], u8)
        MOD = sb("MOD", [P, 48, 2])
        AB = sb("AB", [P, 4, KT, 2])
        cs = sb("cs", [P, KT, 2])
        stat = sb("stat", [P, 16])
        DEC = sb("DEC", [P, 16])
        ST = sb("ST", [P, B_HEADS, P])
        rows = sb("rows", [16, 6, T])
        qw = sb("qw", [P, 1])
        acol = sb("acol", [P, 2, ML_HEADS])
        rt = sb("rt", [P, 2, 64])
        rsel = sb("rsel", [P, 2, 2, N_EXPERTS])
        widx = sb("widx", [P, 2, 8], u32)
        wrow = sb("wrow", [N_EXPERTS, T])
        GW = sb("GW", [P, T])
        many = sb("many", [P, N_EXPERTS], mybir.dt.int32)
        B = [ctx.enter_context(nc.psum_tensor(f"bank{i}", [P, 512], f32)) for i in range(8)]

        def C(name, width):
            return cst[:, CONSTS[name]:CONSTS[name] + width]

        def W(name, width):
            return par[:, PARAMS[name]:PARAMS[name] + width]

        ident, mean_d, mean_dk, mean_dh = C("ident", P), C("mean_d", P), C("mean_dk", P), C("mean_dh", P)
        ones = C("ones", P)
        eps = C("eps", 1)
        nsel = C("nsel", 12)

        def flat(ap):
            return ap.rearrange("p a b -> p (a b)")

        slot_full = [S(f"slot{i}_full") for i in range(NSLOT)]
        unit_done = S("unit_done")
        lin_free = S("lin_free")

        class Chain:

            def __init__(self, eng, name):
                self.eng, self.sem, self.n, self.off = eng, S(name), 0, 0

            def __call__(self, ins):
                self.n += 1
                ins.then_inc(self.sem, 1)
                self.eng.wait_ge(self.sem, self.n + self.off)

        tile_base, tb = {}, 0
        ntiles = {"mod0": 0, "mod1": 0, "proj0": 22 + 12, "proj1": 16 + 16, "moe_up": N_EXPERTS * 2 * ET, "moe_down": N_EXPERTS * KT}
        for l in range(DEPTH):
            ntiles |= {f"wout{l}": 8, f"up{l}": 2 * FT, f"down{l}": KT, f"tproj{l}": 24 + 8, f"gates{l}": 24,
                       f"branch{l}": 24, f"twout{l}": 8}
        ntiles |= {"swup": 2 * FT, "swdown": KT}
        for name, _, _ in STAGES:
            tile_base[name] = tb
            tb += ntiles[name]

        def slot_of(u):
            return u % NSLOT

        BIAS = PROJ[:, 22 * TC:24 * TC].rearrange("p (h n) -> p h n", h=2)

        def proj0(i):
            return PROJ[:, i * TC:(i + 1) * TC]

        K1 = PROJ[:, 2048:6144].rearrange("p (k t) -> p k t", t=TC)
        Q1 = PROJ[:, 0:2048].rearrange("p (k t) -> p k t", t=T)
        V1 = PROJ[:, 6144:10240].rearrange("p (k n) -> p k n", n=D)
        AV = VT[:, 0:512].rearrange("p (k n) -> p k n", n=P)
        BI = VT[:, 512:2560].rearrange("p (k n) -> p k n", n=512)
        P2 = PROJ[:, 0:24 * T].rearrange("p (k t) -> p k t", t=T)
        G2 = PROJ[:, 24 * T:48 * T].rearrange("p (k t) -> p k t", t=T)
        V2 = VT[:, 0:2048].rearrange("p (k n) -> p k n", n=D)
        BR = rows[0:12, 3, :]

        ATT = []
        for h in range(A_HEADS):
            lo = DH * (h % 2)
            g = h // (A_HEADS // A_KV)
            for qt in range(4):
                q = proj0(h // 2)[lo:lo + DH, qt * P:(qt + 1) * P]
                kt = range(4) if qt < 2 else range(2, 4)
                k = proj0(4 + g)[lo:lo + DH, kt[0] * P:(kt[-1] + 1) * P]
                ATT.append((0, h, qt, q, k, [AV[:, j, g * DH:(g + 1) * DH] for j in kt],
                            MIX[lo:lo + DH, h // 2, qt * P:(qt + 1) * P]))
        for h in range(C_HEADS):
            lo = DH * (h % 2)
            for qt in range(2):
                ATT.append((1, h, qt, Q1[lo:lo + DH, h // 2, qt * P:(qt + 1) * P], K1[lo:lo + DH, h // 2, :],
                            [V1[:, j, h * DH:(h + 1) * DH] for j in range(4)],
                            MIX[lo:lo + DH, h // 2, qt * P:(qt + 1) * P]))
        for l in range(DEPTH):
            for h in range(FOX_HEADS):
                lo = DH * (h % 2)
                for qt in range(2):
                    ATT.append((2 + l, h, qt, P2[lo:lo + DH, 16 + h // 2, qt * P:(qt + 1) * P],
                                P2[lo:lo + DH, 20 + h // 2, 0:(qt + 1) * P],
                                [V2[:, j, 512 + h * DH:512 + (h + 1) * DH] for j in range(qt + 1)],
                                MIX[lo:lo + DH, 4 + h // 2, T + qt * P:T + (qt + 1) * P]))
        att_of = [[u for u in range(len(ATT)) if ATT[u][0] == l] for l in range(4)]

        def mix_ml(h):
            return MIX[:, h, 0:T]

        def mix_fox(h):
            return MIX[:, 4 + h, T:TC]

        def mix_pool(g):
            return MIX[:, 4 + g, 0:T]

        HK = Y[:, 0:4, :]
        HB = Y[:, 4:8, :]
        HX = [H[:, 0:4, :], H[:, 4:8, :]]
        HKT = HB
        SCv = SC[:, :].rearrange("p (h t) -> p h t", t=TC)
        HQ = PROJ[:, 6 * TC:10 * TC].rearrange("p (h t) -> p h t", t=TC)
        HZ = [PROJ[:, (10 + 4 * d) * TC:(14 + 4 * d) * TC].rearrange("p (h t) -> p h t", t=TC) for d in range(2)]
        HG = PROJ[:, 18 * TC:22 * TC].rearrange("p (h t) -> p h t", t=TC)
        ORDER = [(2, 3, 0, 1), (3, 2, 1, 0)]

        CONV = SC[:, :].rearrange("p (b s t) -> p b s t", b=2, s=2)

        def hid(width):
            return lambda i: PROJ[:, bass.ds(i * width, width)] if not isinstance(i, int) else PROJ[:, i * width:(i + 1) * width]

        WD = flat(Y[0:N_EXPERTS, 0:4, :])

        HTOK = flat(MIX[:, 0:4, :]).rearrange("p (j d) -> p j d", d=D)
        XG = flat(MIX[:, 4:6, :])[:, 0:KT * CAP].rearrange("p (k n) -> p k n", n=CAP)
        OG = flat(MIX[:, 6:8, :])[:, 0:KT * CAP].rearrange("p (k n) -> p k n", n=CAP)
        OGT = H[0:CAP, :, T:T + P]
        SEL = Y[:, 4, 0:2 * CAP].rearrange("p (j n) -> p j n", n=CAP)
        SELW = Y[:, 5, 0:2 * CAP].rearrange("p (j n) -> p j n", n=CAP)
        SELT = Y[0:CAP, 6, 0:T]

        MW = flat(Y[:, 0:3, :]).rearrange("p (h t) -> p h t", h=ML_HEADS)
        MP = flat(Y[:, 3:6, :]).rearrange("p (h t) -> p h t", h=ML_HEADS)
        MH = flat(Y[:, 6:8, :]).rearrange("p (h t) -> p h t", h=ML_HEADS)
        PSC = SC[:, :].rearrange("p (a t) -> p a t", t=T)

        block = ctx.enter_context(nc.Block())

        @block.sync
        def _(sp):
            sp.dma_start(cst[:, :], dram["consts"]).then_inc(S("consts_in"), 16)
            sp.dma_start(par[:, :], dram["params"]).then_inc(S("params_in"), 16)
            sp.dma_start(flat(X[:, :, :]), dram["xT"]).then_inc(S("x_in"), 16)

            def stream(name, u0, n, src):
                loops = n // NSLOT

                def one(j, it):
                    u = u0 + j
                    sp.wait_ge(unit_done, it * NSLOT + (u - NSLOT + 1))
                    w = src.shape[-1]
                    sp.dma_start(ring[:, slot_of(u), 0:w], src[it * NSLOT + j]).then_inc(slot_full[slot_of(u)], 16)

                if loops > 1:
                    with sp.Fori(0, loops) as it:
                        for j in range(NSLOT):
                            one(j, it)
                else:
                    loops = 0
                for j in range(loops * NSLOT, n):
                    one(j, 0)

            for name, n, w in STAGES:
                src = dram[name]
                if name == "mod0":
                    for u in range(NSLOT):
                        sp.dma_start(ring[:, u, 0:w], src[u]).then_inc(slot_full[u], 16)
                    stream(name, NSLOT, n - NSLOT, src[NSLOT:n])
                elif name == "moe_up":
                    with sp.Fori(0, N_EXPERTS) as e:
                        with sp.Fori(0, ET // NSLOT) as it:
                            for j in range(NSLOT):
                                u = MOE0 + j
                                sp.wait_ge(unit_done, e * PER_E + it * NSLOT + (u - NSLOT + 1))
                                sp.dma_start(ring[:, slot_of(u), :], src[e * ET + it * NSLOT + j])\
                                  .then_inc(slot_full[slot_of(u)], 16)
                        with sp.Fori(0, 16 // NSLOT) as it:
                            for j in range(NSLOT):
                                u = MOE0 + ET + j
                                sp.wait_ge(unit_done, e * PER_E + it * NSLOT + (u - NSLOT + 1))
                                sp.dma_start(ring[:, slot_of(u), 0:EDOWN_W], dram["moe_down"][e * 16 + it * NSLOT + j])\
                                  .then_inc(slot_full[slot_of(u)], 16)
                elif name != "moe_down":
                    stream(name, base[name], n, src)
            sp.wait_ge(S("out_ready"), KT)
            sp.dma_start(out, Y[:, :, 0:T]).then_inc(S("out_written"), 16)
            sp.wait_ge(S("out_written"), 16)

        @block.tensor
        def _(pe):
            def unit(u, it=0):
                pe.wait_ge(slot_full[slot_of(u)], it * 16 + 16 * (u // NSLOT + 1))
                return ring[:, slot_of(u), :]

            def norm(n, width):
                for k in range(KT):
                    pe.wait_ge(S(f"norm{n}_sq"), k + 1)
                    mm = pe.matmul(B[4][:, 0:width], mean_d, H[:, k, 0:width], start=k == 0, stop=k == KT - 1)
                mm.then_inc(S("norm_ms"), 1)

            def mod(l):
                if l == 0:
                    pe.wait_ge(S("cs_ready"), 1)
                else:
                    pe.wait_ge(S("mod_ready"), 1)
                u0 = base[f"mod{l}"]
                with pe.Fori(0, 24 // NSLOT) as it:
                    for j in range(NSLOT):
                        w = unit(u0 + j, it).rearrange("p (k n) -> p k n", n=2 * P)
                        for t in range(2):
                            for k in range(KT):
                                mm = pe.matmul(B[5][:, bass.ds(it * (4 * NSLOT) + 4 * j + 2 * t, 2)], w[:, k, t * P:(t + 1) * P],
                                               cs[:, k, :], start=k == 0, stop=k == KT - 1)
                        mm.then_inc(unit_done, 1)

            def fm_unit(u, tile, src, width, it=0, tiles_per_it=0, k_n=KT):
                w = unit(u, it).rearrange("p (k n) -> p k n", n=2 * P)
                for t in range(2):
                    pe.wait_ge(lin_free, it * tiles_per_it + tile + t + 1)
                    for k in range(k_n):
                        mm = pe.matmul(B[(tile + t) % 4][:, 0:width], w[:, k, t * P:(t + 1) * P], src[:, k, 0:width],
                                       start=k == 0, stop=k == k_n - 1)
                mm.then_inc(unit_done, 1)

            def fm_unit_at(u, tile, src, lo, width):
                w = unit(u).rearrange("p (k n) -> p k n", n=2 * P)
                for t in range(2):
                    pe.wait_ge(lin_free, tile + t + 1)
                    for k in range(KT):
                        mm = pe.matmul(B[(tile + t) % 4][:, 0:width], w[:, k, t * P:(t + 1) * P], src[:, k, lo:lo + width],
                                       start=k == 0, stop=k == KT - 1)
                mm.then_inc(unit_done, 1)

            def tm_unit(u, tile, tts):
                w = unit(u).rearrange("p (k n) -> p k n", n=2 * P)
                for t in range(tts):
                    pe.wait_ge(lin_free, tile + t + 1)
                    for k in range(KT):
                        mm = pe.matmul(B[(tile + t) % 4][:, 0:2 * P], H[:, k, t * P:(t + 1) * P], w[:, k, :],
                                       start=k == 0, stop=k == KT - 1)
                mm.then_inc(unit_done, 1)

            def wout(name, src, width):
                for j in range(4):
                    fm_unit(base[name] + j, tile_base[name] + 2 * j, src, width)

            def pairs(name, width, k_n=KT):
                u0, t0, n = base[name], tile_base[name], FT
                loops = n // NSLOT
                with pe.Fori(0, loops) as it:
                    for j in range(NSLOT):
                        fm_unit(u0 + j, t0 + 2 * j, H, width, it, 2 * NSLOT)
                for j in range(loops * NSLOT, n):
                    fm_unit(u0 + j, t0 + 2 * j, H, width)

            def down_tile(u, tile, bank, src, width, half, it=0, e_units=0, units_it=NSLOT, tiles_it=NSLOT // 2, e=None, e_tiles=0):
                wait = it * tiles_it + tile + 3
                pe.wait_ge(lin_free, wait if e is None else wait + e * e_tiles)
                for s in range(2):
                    uu = u + s
                    rounds = it * (units_it // NSLOT)
                    if e is not None:
                        rounds = rounds + e * (e_units // NSLOT)
                    pe.wait_ge(slot_full[slot_of(uu)], rounds * 16 + 16 * (uu // NSLOT + 1))
                    w = ring[:, slot_of(uu), 0:half * P].rearrange("p (k n) -> p k n", n=P)
                    for k in range(half):
                        mm = pe.matmul(B[bank][:, 0:width], w[:, k, :], src(s * half + k),
                                       start=s == 0 and k == 0, stop=s == 1 and k == half - 1)
                    mm.then_inc(unit_done, 1)

            def down(name, width):
                h = hid(width)
                with pe.Fori(0, 16 // NSLOT) as it:
                    for j in range(NSLOT // 2):
                        down_tile(base[name] + 2 * j, tile_base[name] + j, j % 2, h, width, FT // 2, it)

            def attention(l):
                us = att_of[l]
                n0 = us[0]

                def scores(u):
                    _, h, qt, q, k, v, _ = ATT[u]
                    if u >= n0 + 2:
                        pe.wait_ge(S("att_exp"), u - 1)
                    if l == 1 and qt == 0:
                        pe.wait_ge(S(f"bias{h % 2}_in"), 16 * (h // 2 + 1))
                    s, nk = B[u % 2], len(v) * P
                    mm = pe.matmul(s[:, 0:nk], q, k, start=True, stop=l == 0)
                    if l == 1:
                        mm = pe.matmul(s[:, 0:T], ident, BIAS[:, h % 2, qt * T:(qt + 1) * T], start=False, stop=True)
                    if l >= 2:
                        pe.matmul(s[:, 0:nk], nsel[0:12, ML_HEADS + h:ML_HEADS + h + 1].to_broadcast([12, P]), BR[:, 0:nk], start=False, stop=False)
                        mm = pe.matmul(s[:, qt * P:nk], ident, C("causal_add", P), start=False, stop=True)
                    mm.then_inc(S("att_s"), 1)

                def turn(u):
                    pe.wait_ge(S("att_p"), u + 1)
                    if u >= n0 + 2:
                        pe.wait_ge(S("att_ptc"), u - 1)
                    for j in range(len(ATT[u][5])):
                        mm = pe.transpose(B[2 + u % 2][:, j * P:(j + 1) * P], PR[:, u % 2, j * P:(j + 1) * P], ident)
                    mm.then_inc(S("att_t"), 1)

                def values(u):
                    v = ATT[u][5]
                    pe.wait_ge(S("att_ptc"), u + 1)
                    if u >= n0 + 2:
                        pe.wait_ge(S("att_oc"), u - 1)
                    lo = DH * (ATT[u][1] % 2)
                    for j in range(len(v)):
                        mm = pe.matmul(B[6 + u % 2][lo:lo + DH, 0:P], v[j], PTB[:, u % 2, j * P:(j + 1) * P],
                                       start=j == 0, stop=j == len(v) - 1)
                    mm.then_inc(S("att_o"), 1)

                n = len(us)
                for i in range(n + 2):
                    if i < n:
                        scores(us[i])
                    if 1 <= i <= n:
                        turn(us[i - 1])
                    if i >= 2:
                        values(us[i - 2])

            def gqa_prep():
                for i in range(6):
                    pe.wait_ge(S("gqa_sq"), i + 1)
                    if i >= 1:
                        pe.wait_ge(S("gqa_rt"), i)
                    pe.matmul(B[4][:, 0:TC], mean_dh, H[:, i, :], start=True, stop=True).then_inc(S("gqa_ms"), 1)
                    pe.wait_ge(S("gqa_n"), i + 1)
                    if i >= 1:
                        pe.wait_ge(S("gqa_rot"), i)
                    pe.matmul(B[5][:, 0:T], C("swap", P), proj0(i)[:, 0:T], start=True, stop=True).then_inc(S("gqa_sw"), 1)

            def hgrn(d):
                nl = len(LEVELS)
                for i in range(nl):
                    if i == 0:
                        pe.wait_ge(S("hg_k"), d + 1)
                        pe.wait_ge(S("hg_q"), 1)
                    else:
                        pe.wait_ge(S("hg_x"), d * (nl - 1) + i)
                    for h in range(B_HEADS):
                        n = d * nl * B_HEADS + i * B_HEADS + h
                        if i > 0:
                            pe.wait_ge(S("hg_cp"), n - B_HEADS + 1)
                        for c in range(4):
                            cols = slice(c * P, (c + 1) * P)
                            a, b = (HK[:, h, cols], HQ[:, h, cols]) if i == 0 else (HX[i % 2][:, h, cols],) * 2
                            mm = pe.matmul(B[h][:, cols], a, b, start=True, stop=True)
                        mm.then_inc(S("hg_mm"), 1)
                for h in range(B_HEADS):
                    pe.wait_ge(S("hg_cp"), (d * nl + nl - 1) * B_HEADS + h + 1)
                    for c in range(4):
                        pe.matmul(B[4 + h][:, c * P:(c + 1) * P], BI[:, c, h * P:(h + 1) * P], SCv[:, h, c * P:(c + 1) * P],
                                  start=d == 0 and c == 0, stop=False, skip_group_check=True)
                pe.wait_ge(S("hg_kt"), d + 1)
                for h in range(B_HEADS):
                    for c in range(4):
                        mm = pe.transpose(B[h][:, c * P:(c + 1) * P], HX[1][:, h, c * P:(c + 1) * P], ident)
                    mm.then_inc(S("hg_ktt"), 1)
                for i, c in enumerate(ORDER[d]):
                    for h in range(B_HEADS):
                        if i > 0:
                            pe.wait_ge(S("hg_s"), d * 3 * B_HEADS + (i - 1) * B_HEADS + h + 1)
                            mm = pe.matmul(B[4 + h][:, c * P:(c + 1) * P], ST[:, h, :], HX[0][:, h, c * P:(c + 1) * P],
                                           start=False, stop=d == 1 and i == 3, skip_group_check=True)
                        if i < 3:
                            pe.wait_ge(S("hg_ktc"), d * B_HEADS + h + 1)
                            mm = pe.matmul(B[h][:, 0:P], HKT[:, h, c * P:(c + 1) * P], BI[:, c, h * P:(h + 1) * P],
                                           start=True, stop=True)
                            mm.then_inc(S("hg_u"), 1)
                mm.then_inc(S("hg_done"), 1)

            def hgrn_norm():
                for h in range(B_HEADS):
                    pe.wait_ge(S("hg_sq"), h + 1)
                    pe.matmul(B[h][:, 0:TC], mean_dk, H[:, h, :], start=True, stop=True).then_inc(S("hg_ms"), 1)

            def small_gates(l):
                ws = W(f"w_small{l}", KT * 16).rearrange("p (k n) -> p k n", n=16)
                for lo, n, col in ((0, 4, 0), (4, 12, T)):
                    for k in range(KT):
                        mm = pe.matmul(B[5][0:n, col:col + T], ws[:, k, lo:lo + n], H[:, k, 0:T], start=k == 0, stop=k == KT - 1)
                mm.then_inc(S("sg_mm"), 1)

            def pool(l):
                wg = W(f"w_grp{l}", 4 * P).rearrange("p (g n) -> p g n", n=P)
                pe.wait_ge(S("pool_d"), 4 * l + 4)
                for g in range(4):
                    mm = pe.matmul(B[4 + g // 2][:, (g % 2) * T:(g % 2 + 1) * T], wg[:, g, :], P2[:, g, :], start=True, stop=True)
                mm.then_inc(S("pool_mm"), 1)

            def mlstm(l):
                pe.wait_ge(S("ml_rows"), l + 1)
                for j in range(2):
                    mm = pe.transpose(B[4][:, ML_HEADS * j:ML_HEADS * (j + 1)], rows[0:4, 4, j * P:(j + 1) * P], ident[0:4, 0:4])
                mm.then_inc(S("ml_at"), 1)
                for h in range(ML_HEADS):
                    if h == 0:
                        pe.wait_ge(S("ml_acol"), l + 1)
                    pe.matmul(B[4 + h][:, 0:T], nsel[0:4, h:h + 1].to_broadcast([4, P]), rows[0:4, 5, :], start=True, stop=True)
                    pe.matmul(B[4 + h][:, T:TC], nsel[0:4, h:h + 1].to_broadcast([4, P]), rows[0:4, 2, :], start=True, stop=True).then_inc(S("ml_bc"), 1)
                    pe.matmul(B[h][:, 0:T], P2[:, 8 + h, 0:P], P2[:, 4 + h, :], start=True, stop=True)
                    pe.matmul(B[h][:, T:T + P], P2[:, 8 + h, P:T], P2[:, 4 + h, P:T], start=True, stop=True).then_inc(S("ml_s"), 1)
                for h in range(ML_HEADS):
                    pe.wait_ge(S("ml_p"), ML_HEADS * l + h + 1)
                    for col, left in ((0, lambda j: V2[:, j, h * P:(h + 1) * P]), (T, lambda j: ones)):
                        pe.matmul(B[h][:, col:col + T], left(0), MP[:, h, 0:T], start=True, stop=False)
                        mm = pe.matmul(B[h][:, col + P:col + T], left(1), MP[:, h, T:T + P], start=False, stop=True)
                    mm.then_inc(S("ml_nd"), 1)
                for h in range(ML_HEADS):
                    pe.wait_ge(S("ml_sq"), ML_HEADS * l + h + 1)
                    pe.matmul(B[4 + h][:, 0:T], mean_dk, MW[:, h, 0:T], start=True, stop=True).then_inc(S("ml_ms"), 1)

            def branch(l):
                for j in range(KT):
                    u = base[f"branch{l}"] + j
                    w = unit(u)[:, 0:12 * P].rearrange("p (b k n) -> p b k n", b=3, n=P)
                    for b, src in enumerate((mix_pool, mix_ml, mix_fox)):
                        tile = tile_base[f"branch{l}"] + 3 * j + b
                        pe.wait_ge(lin_free, tile + 1)
                        for k in range(4):
                            mm = pe.matmul(B[tile % 4][:, 0:T], w[:, b, k, :], src(k), start=k == 0, stop=k == 3)
                    mm.then_inc(unit_done, 1)

            def router():
                wr = W("w_router", KT * N_EXPERTS).rearrange("p (k n) -> p k n", n=N_EXPERTS)
                for j in range(2):
                    for k in range(KT):
                        mm = pe.matmul(B[5][:, 8 * j:8 * j + 8], H[:, k, j * P:(j + 1) * P], wr[:, k, :], start=k == 0, stop=k == KT - 1)
                mm.then_inc(S("rt_mm"), 1)
                pe.wait_ge(S("rt_w"), 2)
                for j in range(2):
                    mm = pe.transpose(B[6][0:N_EXPERTS, j * P:(j + 1) * P], rt[:, j, 48:56], ident)
                mm.then_inc(S("rt_t"), 1)

            def moe():
                pe.wait_ge(S("rt_wr"), 1)
                for j in range(2):
                    for k in range(KT):
                        mm = pe.transpose(B[2 * j + k // 4][:, (k % 4) * P:(k % 4 + 1) * P], H[:, k, j * P:(j + 1) * P], ident)
                mm.then_inc(S("mo_h"), 1)
                for j in range(2):
                    pe.matmul(B[5][:, 32 + 8 * j:40 + 8 * j], C("causal_mul", P), rt[:, j, 24:32], start=True, stop=j == 0)
                pe.matmul(B[5][:, 40:48], ones, rt[:, 0, 24:32], start=False, stop=True)
                pe.matmul(B[5][:, 48:56], ones, rt[:, 0, 24:32], start=True, stop=False)
                pe.matmul(B[5][:, 48:56], ones, rt[:, 1, 24:32], start=False, stop=True).then_inc(S("mo_n"), 1)
                pe.wait_ge(S("mo_many"), 1)
                pe.wait_ge(S("mo_hc"), 4)
                t0, per_t = tile_base["moe_up"], 2 * ET + KT

                def expert(e, src, hidden, n):
                    with pe.Fori(0, ET // NSLOT) as it:
                        for j in range(NSLOT):
                            u = MOE0 + j
                            pe.wait_ge(slot_full[slot_of(u)], e * (16 * PER_E // NSLOT) + it * 16 + 16 * (u // NSLOT + 1))
                            w = ring[:, slot_of(u), :].rearrange("p (k n) -> p k n", n=2 * P)
                            for t in range(2):
                                pe.wait_ge(lin_free, e * per_t + it * (2 * NSLOT) + (t0 + 2 * j + t + 1))
                                for k in range(KT):
                                    mm = pe.matmul(B[(t0 + 2 * j + t) % 4][:, 0:n], w[:, k, t * P:(t + 1) * P], src[:, k, 0:n],
                                                   start=k == 0, stop=k == KT - 1)
                            mm.then_inc(unit_done, 1)
                    with pe.Fori(0, 16 // NSLOT) as it:
                        pe.wait_ge(lin_free, e * per_t + (t0 + 2 * ET + 4))
                        for j in range(NSLOT // 2):
                            down_tile(MOE0 + ET + 2 * j, t0 + 2 * ET + j, j % 2, hidden, n, ET // 2, it, PER_E, e=e, e_tiles=per_t)

                with pe.Fori(0, N_EXPERTS) as e:
                    pe.wait_ge(S("mo_sel"), e + 1)
                    pe.matmul(B[5][:, T:TC], ones[0:N_EXPERTS, :], WD[:, bass.ds(e * T, T)], start=True, stop=True)
                    for j in range(2):
                        mm = pe.transpose(B[5][0:CAP, j * P:(j + 1) * P], SELW[:, j, :], ident)
                    mm.then_inc(S("mo_a"), 1)
                    pe.wait_ge(S("mo_sc"), e * 4 + 4)
                    for k in range(KT):
                        for j in range(2):
                            mm = pe.matmul(B[6 + k // 4][:, (k % 4) * CAP:(k % 4 + 1) * CAP], HTOK[:, j, k * P:(k + 1) * P],
                                           SEL[:, j, :], start=j == 0, stop=j == 1)
                    mm.then_inc(S("mo_g"), 1)
                    pe.wait_ge(S("mo_xg"), e * 2 + 2)
                    dense = pe.value_load(many[0:1, bass.ds(e, 1)], min_val=0, max_val=1)
                    with pe.If(dense):
                        expert(e, H, hid(T), T)
                        pe.sem_inc(S("mo_t"), 2)
                        pe.sem_inc(S("mo_s"), 4)
                    with pe.Else():
                        expert(e, XG, hid(CAP), CAP)
                        pe.wait_ge(lin_free, e * per_t + (t0 + per_t + 4))
                        for k in range(KT):
                            mm = pe.transpose(B[6 + k // 4][0:CAP, (k % 4) * P:(k % 4 + 1) * P], OG[:, k, :], ident)
                            if k % 4 == 3:
                                mm.then_inc(S("mo_t"), 1)
                        pe.wait_ge(S("mo_selt"), e + 1)
                        pe.wait_ge(S("mo_tc"), e * 2 + 2)
                        for i in range(4):
                            if i >= 2:
                                pe.wait_ge(S("mo_sc"), e * 4 + (4 + i - 1))
                            for k in range(2):
                                mm = pe.matmul(B[6 + i % 2][:, k * T:(k + 1) * T], OGT[:, 2 * i + k, :], SELT, start=True, stop=True)
                            mm.then_inc(S("mo_s"), 1)

            pe.wait_ge(S("consts_in"), 16)
            pe.wait_ge(S("params_in"), 16)
            mod(0)
            norm(0, TC)
            pe.wait_ge(S("norm0_out"), 16)
            u0, t0 = base["proj0"], tile_base["proj0"]
            for j in range(11):
                fm_unit(u0 + j, t0 + 2 * j, H, TC)
            for j in range(3):
                tm_unit(u0 + 11 + j, t0 + 22 + 4 * j, 4)
            gqa_prep()
            pe.wait_ge(S("gqa_rot"), 6)
            pe.wait_ge(lin_free, t0 + 34 + 4)
            attention(0)
            pe.wait_ge(S("att_oc"), att_of[0][-1] + 1)
            hgrn(0)
            hgrn(1)
            hgrn_norm()
            pe.wait_ge(S("hg_mix"), 4)
            wout("wout0", MIX, TC)
            norm(1, TC)
            norm(2, TC)
            pe.wait_ge(S("norm2_out"), 16)
            pairs("up0", TC)
            pe.wait_ge(S("ffn_hid"), FT + 2)
            down("down0", TC)
            norm(3, TC)
            mod(1)
            norm(4, TC)
            pe.wait_ge(S("norm4_out"), 16)
            u0, t0 = base["proj1"], tile_base["proj1"]
            for j in range(4):
                fm_unit(u0 + j, t0 + 2 * j, H, T)
            for j in range(4):
                fm_unit(u0 + 4 + j, t0 + 8 + 2 * j, H, TC)
            for j in range(4):
                tm_unit(u0 + 8 + j, t0 + 16 + 4 * j, 4)
            pe.wait_ge(lin_free, t0 + 32 + 4)
            attention(1)
            pe.wait_ge(S("att_oc"), att_of[1][-1] + 1)
            wout("wout1", MIX, T)
            norm(5, T)
            norm(6, T)
            pe.wait_ge(S("norm6_out"), 8)
            pairs("up1", T)
            pe.wait_ge(S("ffn_hid"), 2 * FT + 2)
            down("down1", T)
            norm(7, T)
            for l in range(DEPTH):
                norm(8 + 2 * l, T)
                pe.wait_ge(S(f"norm{8 + 2 * l}_out"), 8)
                u0, t0 = base[f"tproj{l}"], tile_base[f"tproj{l}"]
                small_gates(l)
                for j in range(12):
                    fm_unit(u0 + j, t0 + 2 * j, H, T)
                for j in range(4):
                    tm_unit(u0 + 12 + j, t0 + 24 + 2 * j, 2)
                for j in range(12):
                    fm_unit(base[f"gates{l}"] + j, tile_base[f"gates{l}"] + 2 * j, H, T)
                pe.wait_ge(lin_free, tile_base[f"gates{l}"] + 24 + 4)
                mlstm(l)
                pe.wait_ge(S("ml_mix"), 4 * l + 4)
                attention(2 + l)
                pe.wait_ge(S("att_oc"), att_of[2 + l][-1] + 1)
                pool(l)
                pe.wait_ge(S("pool_mix"), 4 * l + 4)
                branch(l)
                pe.wait_ge(S("merged"), 8 * l + 8)
                wout(f"twout{l}", H[:, :, T:TC], T)
                norm(9 + 2 * l, T)
                pe.wait_ge(S(f"norm{9 + 2 * l}_out"), 8)
                if l == 0:
                    pairs("swup", T)
                    pe.wait_ge(lin_free, tile_base["swup"] + 2 * FT + 4)
                    down("swdown", T)
            router()
            moe()
            norm(12, T)

        @block.scalar
        def _(act):
            step = Chain(act, "act_step")

            def squares(n, src, width, sem, first, every):
                for k in range(KT):
                    act.wait_ge(sem, first + every * k)
                    act.activation(H[:, k, 0:width], src[:, k, 0:width], ACT.Square).then_inc(S(f"norm{n}_sq"), 1)

            def root(n, width):
                act.wait_ge(S("norm_ms"), n + 1)
                act.activation(RT[:, 0:width], B[4][:, 0:width], ACT.Sqrt, bias=eps).then_inc(S("norm_rt"), 1)

            def shift(n, sh, width):
                for k in range(KT):
                    for s in range(width // T):
                        act.wait_ge(S(f"norm{n}_scaled"), k * (width // T) + s + 1)
                        part = H[:, k, s * T:(s + 1) * T]
                        act.activation(part, part, ACT.Identity, bias=MOD[:, sh + k, s:s + 1]).then_inc(S(f"norm{n}_out"), 1)

            def copy_out(name, tile, unit, dst, src_cols, func=ACT.Copy, scale=1.0):
                act.wait_ge(unit_done, base[name] + unit + 1)
                act.activation(dst, B[(tile_base[name] + tile) % 4][:, 0:src_cols], func, scale=scale).then_inc(lin_free, 1)

            def to_y(name, width):
                for k in range(KT):
                    copy_out(name, k, k // 2, Y[:, k, 0:width], width)

            def down_to_y(name, width):
                u0 = base[name]
                with act.Fori(0, 16 // NSLOT) as it:
                    for j in range(NSLOT // 2):
                        act.wait_ge(unit_done, it * NSLOT + (u0 + 2 * j + 2))
                        dst = Y[:, bass.ds(it * (NSLOT // 2) + j, 1), 0:width].rearrange("p a t -> p (a t)")
                        act.activation(dst, B[j % 2][:, 0:width], ACT.Copy).then_inc(lin_free, 1)

            def conv_ffn(l, width):
                name = f"up{l}"
                u0, t0 = base[name], tile_base[name]
                cw = W(f"conv{l}", 2 * FT * 4)

                def pair(j, it):
                    act.wait_ge(unit_done, it * NSLOT + (u0 + j + 1))
                    act.wait_ge(S("ffn_hid"), it * NSLOT + (l * FT + j + 1))
                    for t in range(2):
                        col = lambda w: cw[:, bass.ds(it * (4 * NSLOT) + 4 * (t * FT + j) + w, 1)]
                        mm = act.activation(CONV[:, j % 2, t, 0:width], B[(t0 + 2 * j + t) % 4][:, 0:width], ACT.Identity,
                                            bias=col(3), scale=col(1))
                    mm.then_inc(S("conv_c"), 1)
                    act.wait_ge(S("conv_d"), it * NSLOT + (l * FT + j + 1))
                    g = CONV[:, j % 2, 1, 0:width]
                    act.activation(g, g, ACT.Silu).then_inc(lin_free, 2)

                loops = FT // NSLOT
                with act.Fori(0, loops) as it:
                    for j in range(NSLOT):
                        pair(j, it)
                for j in range(loops * NSLOT, FT):
                    pair(j, 0)

            def attention(l):
                us = att_of[l]
                n0 = us[0]

                def exps(u):
                    nk = len(ATT[u][5]) * P
                    act.wait_ge(S("att_m"), u + 1)
                    if u >= n0 + 2:
                        act.wait_ge(S("att_t"), u - 1)
                    act.activation(PR[:, u % 2, 0:nk], B[u % 2][:, 0:nk], ACT.Exp, bias=stat[:, u % 4:u % 4 + 1],
                                   accum_out=stat[:, 4 + u % 4:5 + u % 4]).then_inc(S("att_exp"), 1)

                def turned(u):
                    nk = len(ATT[u][5]) * P
                    act.wait_ge(S("att_t"), u + 1)
                    if u >= n0 + 2:
                        act.wait_ge(S("att_o"), u - 1)
                    act.activation(PTB[:, u % 2, 0:nk], B[2 + u % 2][:, 0:nk], ACT.Copy).then_inc(S("att_ptc"), 1)

                for i in range(len(us) + 1):
                    if i < len(us):
                        exps(us[i])
                    if i >= 1:
                        turned(us[i - 1])

            def gqa_prep():
                act.wait_ge(unit_done, base["proj0"] + 14)
                for i in range(6):
                    act.wait_ge(lin_free, tile_base["proj0"] + i + 1 + 4)
                    act.activation(H[:, i, :], proj0(i), ACT.Square).then_inc(S("gqa_sq"), 1)
                    act.wait_ge(S("gqa_ms"), i + 1)
                    if i >= 1:
                        act.wait_ge(S("gqa_n"), i)
                    act.activation(RT[:, :], B[4][:, 0:TC], ACT.Sqrt, bias=eps).then_inc(S("gqa_rt"), 1)

            def hgrn(d):
                nl = len(LEVELS)
                if d == 0:
                    act.wait_ge(lin_free, tile_base["proj0"] + 34 + 4)
                    act.wait_ge(S("gqa_ms"), 6)
                else:
                    act.wait_ge(S("hg_done"), d)
                act.activation(HK, HZ[d], ACT.Sigmoid, scale=-1.0).then_inc(S("hg_k"), 1)
                step(act.activation(HX[0], HZ[d], ACT.Abs))
                step(act.activation(HX[0], HX[0], ACT.Exp, scale=-1.0))
                act.activation(HX[0], HX[0], ACT.Ln, bias=1.0).then_inc(S("hg_ln"), 1)
                for i in range(1, nl):
                    act.wait_ge(S("hg_d"), d * (nl - 1) + i)
                    act.activation(HX[i % 2], HX[i % 2], ACT.Exp).then_inc(S("hg_e"), 1)
                act.wait_ge(S("hg_mm"), (d * nl + 7) * B_HEADS)
                act.activation(HX[0], HB, ACT.Exp).then_inc(S("hg_e0"), 1)
                act.wait_ge(S("hg_dk"), d + 1)
                act.activation(HX[1], HX[1], ACT.Exp).then_inc(S("hg_ek"), 1)
                for h in range(B_HEADS):
                    act.wait_ge(S("hg_ktt"), d * B_HEADS + h + 1)
                    act.activation(HKT[:, h, :], B[h][:, :], ACT.Copy).then_inc(S("hg_ktc"), 1)

            def hgrn_norm():
                act.wait_ge(S("hg_done"), 2)
                for h in range(B_HEADS):
                    act.activation(H[:, h, :], B[4 + h][:, :], ACT.Square).then_inc(S("hg_sq"), 1)
                for h in range(B_HEADS):
                    act.wait_ge(S("hg_ms"), h + 1)
                    act.activation(SCv[:, h, :], B[h][:, :], ACT.Sqrt, bias=eps).then_inc(S("hg_rt"), 1)

            def gate_rows(l):
                act.wait_ge(S("sg_mm"), l + 1)
                act.activation(rows[0:4, 0, :], B[5][0:4, 0:T], ACT.Identity, bias=W(f"b_i{l}", 1)[0:4])
                step(act.activation(rows[0:12, 1, :], B[5][0:12, T:TC], ACT.Abs, bias=W(f"b_f{l}", 1)[0:12]))
                step(act.activation(rows[0:12, 1, :], rows[0:12, 1, :], ACT.Exp, scale=-1.0))
                act.activation(rows[0:12, 1, :], rows[0:12, 1, :], ACT.Ln, bias=1.0).then_inc(S("ml_ln"), 1)
                act.wait_ge(S("ml_bm"), l + 1)
                act.activation(rows[0:4, 2, :], rows[0:4, 2, :], ACT.Exp, scale=-1.0).then_inc(S("ml_rows"), 1)

            def mlstm(l):
                for h in range(ML_HEADS):
                    act.wait_ge(S("ml_w"), ML_HEADS * l + h + 1)
                    act.activation(MW[:, h, :], MW[:, h, :], ACT.Exp).then_inc(S("ml_e"), 1)
                for h in range(ML_HEADS):
                    act.wait_ge(S("ml_h"), ML_HEADS * l + h + 1)
                    act.activation(MW[:, h, 0:T], MH[:, h, :], ACT.Square).then_inc(S("ml_sq"), 1)
                for h in range(ML_HEADS):
                    act.wait_ge(S("ml_ms"), ML_HEADS * l + h + 1)
                    act.activation(MP[:, h, 0:T], B[4 + h][:, 0:T], ACT.Sqrt, bias=eps).then_inc(S("ml_rt"), 1)

            def swiglu(name, width, e=None):
                u0, t0 = base[name], tile_base[name]
                eu = 0 if e is None else e * PER_E
                et = 0 if e is None else e * (2 * ET + KT)
                n = FT if e is None else ET

                def pair(j, it):
                    act.wait_ge(unit_done, it * NSLOT + (u0 + j + 1) + eu)
                    act.wait_ge(lin_free, it * (2 * NSLOT) + (t0 + 2 * j + 2) + et)
                    act.activation(CONV[:, j % 2, 0, 0:width], B[(t0 + 2 * j) % 4][:, 0:width], ACT.Silu).then_inc(S("sw_s"), 1)

                loops = n // NSLOT
                with act.Fori(0, loops) as it:
                    for j in range(NSLOT):
                        pair(j, it)
                for j in range(loops * NSLOT, n):
                    pair(j, 0)

            act.wait_ge(S("params_in"), 16)
            act.wait_ge(S("consts_in"), 16)
            act.activation(flat(cs[:, :, :]), W("c", 2 * KT), ACT.Silu).then_inc(S("cs_ready"), 1)
            act.sem_inc(lin_free, 4)
            squares(0, X, TC, S("x_in"), 16, 0)
            root(0, TC)
            shift(0, 0, TC)
            for i in range(22):
                copy_out("proj0", i, i // 2, proj0(i), TC, ACT.Silu if 6 <= i < 10 or i >= 18 else ACT.Copy)
            for j in range(3):
                for t in range(4):
                    if j < 2:
                        copy_out("proj0", 22 + 4 * j + t, 11 + j, BI[:, t, j * T:(j + 1) * T], T)
                    else:
                        copy_out("proj0", 22 + 4 * j + t, 11 + j, AV[:, t, :], P)
            gqa_prep()
            attention(0)
            hgrn(0)
            hgrn(1)
            hgrn_norm()
            to_y("wout0", TC)
            squares(1, Y, TC, lin_free, tile_base["wout0"] + 5, 1)
            root(1, TC)
            squares(2, X, TC, S("norm1_out"), 1, 1)
            root(2, TC)
            shift(2, 24, TC)
            conv_ffn(0, TC)
            down_to_y("down0", TC)
            squares(3, Y, TC, lin_free, tile_base["down0"] + 5, 1)
            root(3, TC)
            squares(4, X, TC, S("norm3_out"), 1, 1)
            root(4, TC)
            act.wait_ge(S("mod_ready"), 2)
            shift(4, 0, TC)
            for i in range(4 * 2):
                copy_out("proj1", i, i // 2, Q1[:, i, :], T, scale=float(DH) ** -0.5)
            for i in range(4 * 2):
                copy_out("proj1", 8 + i, 4 + i // 2, K1[:, i, :], TC)
            for j in range(4):
                for t in range(4):
                    copy_out("proj1", 16 + 4 * j + t, 8 + j, V1[:, t, j * T:(j + 1) * T], T)
            attention(1)
            to_y("wout1", T)
            squares(5, Y, T, lin_free, tile_base["wout1"] + 5, 1)
            root(5, T)
            squares(6, X, T, S("norm5_out"), 1, 1)
            root(6, T)
            shift(6, 24, T)
            conv_ffn(1, T)
            down_to_y("down1", T)
            squares(7, Y, T, lin_free, tile_base["down1"] + 5, 1)
            root(7, T)
            for l in range(DEPTH):
                if l == 0:
                    squares(8, X, T, S("norm7_out"), 1, 1)
                else:
                    squares(10, X, T, lin_free, tile_base["swdown"] + 5, 1)
                root(8 + 2 * l, T)
                gate_rows(l)
                name = f"tproj{l}"
                for i in range(24):
                    if 4 <= i < 12:
                        act.wait_ge(unit_done, base[name] + i // 2 + 1)
                        w = W(f"ml_conv{l}", 32)
                        act.activation(P2[:, i, :], B[(tile_base[name] + i) % 4][:, 0:T], ACT.Copy,
                                       scale=w[:, 4 * (i - 4) + 3:4 * (i - 4) + 4]).then_inc(S("ml_c"), 1)
                        act.wait_ge(S("ml_cv"), 8 * l + i - 3)
                        act.activation(P2[:, i, :], P2[:, i, :], ACT.Silu).then_inc(lin_free, 1)
                    else:
                        copy_out(name, i, i // 2, P2[:, i, :], T, ACT.Sigmoid if 12 <= i < 16 else ACT.Copy,
                                 float(DH) ** -0.5 if 16 <= i < 20 else 1.0)
                for j in range(4):
                    for t in range(2):
                        copy_out(name, 24 + 2 * j + t, 12 + j, V2[:, t, j * T:(j + 1) * T], T)
                for i in range(24):
                    copy_out(f"gates{l}", i, i // 2, G2[:, i, :], T, ACT.Sigmoid)
                mlstm(l)
                attention(2 + l)
                act.wait_ge(S("pool_mm"), l + 1)
                for g in range(4):
                    act.activation(mix_pool(g), B[4 + g // 2][:, (g % 2) * T:(g % 2 + 1) * T], ACT.Copy,
                                   scale=W(f"pool_scale{l}", 4)[:, g:g + 1]).then_inc(S("pool_mix"), 1)
                squares(9 + 2 * l, X, T, lin_free, tile_base[f"twout{l}"] + 5, 1)
                root(9 + 2 * l, T)
                if l == 0:
                    swiglu("swup", T)
            for j in range(2):
                act.wait_ge(S("rt_d"), j + 1)
                act.activation(rt[:, j, 19:20], rt[:, j, 18:19], ACT.Exp).then_inc(S("rt_e"), 1)
            act.wait_ge(S("mo_h"), 1)
            for j in range(2):
                for i in range(2):
                    act.activation(HTOK[:, j, i * 512:(i + 1) * 512], B[2 * j + i][:, :], ACT.Copy).then_inc(S("mo_hc"), 1)
            act.wait_ge(S("mo_many"), 1)
            with act.Fori(0, N_EXPERTS) as e:
                act.wait_ge(S("mo_g"), e + 1)
                for i in range(2):
                    act.activation(XG[:, 4 * i:4 * i + 4, :], B[6 + i][:, 0:4 * CAP].rearrange("p (k n) -> p k n", n=CAP),
                                   ACT.Copy).then_inc(S("mo_xg"), 1)
                dense = act.value_load(many[0:1, bass.ds(e, 1)], min_val=0, max_val=1)
                with act.If(dense):
                    swiglu("moe_up", T, e)
                    act.sem_inc(S("mo_tc"), 2)
                with act.Else():
                    swiglu("moe_up", CAP, e)
                    with act.Fori(0, 16 // NSLOT) as it:
                        for j in range(NSLOT // 2):
                            act.wait_ge(unit_done, it * NSLOT + (MOE0 + ET + 2 * j + 2) + e * PER_E)
                            dst = OG[:, bass.ds(it * (NSLOT // 2) + j, 1), :].rearrange("p a t -> p (a t)")
                            act.activation(dst, B[j % 2][:, 0:CAP], ACT.Copy).then_inc(lin_free, 1)
                    for i in range(2):
                        act.wait_ge(S("mo_t"), e * 2 + i + 1)
                        act.activation(OGT[:, 4 * i:4 * i + 4, :], B[6 + i][0:CAP, :].rearrange("p (k n) -> p k n", n=P),
                                       ACT.Copy).then_inc(S("mo_tc"), 1)
            act.wait_ge(S("mo_sc"), 4 * N_EXPERTS + 4)
            squares(12, X, T, lin_free, tile_base["moe_down"] + KT * N_EXPERTS + 4, 0)
            root(12, T)

        @block.vector
        def _(dve):
            step = Chain(dve, "dve_step")

            def recip_root(n, width):
                dve.wait_ge(S("norm_rt"), n + 1)
                step(dve.reciprocal(RT[:, 0:width], RT[:, 0:width]))

            def modulate(n, row, width):
                recip_root(n, width)
                for k in range(KT):
                    for s in range(width // T):
                        cols = slice(s * T, (s + 1) * T)
                        dve.scalar_tensor_tensor(out=H[:, k, cols], in0=X[:, k, cols], scalar=AB[:, row, k, s:s + 1],
                                                 in1=RT[:, cols], op0=ALU.mult, op1=ALU.mult).then_inc(S(f"norm{n}_scaled"), 1)

            def gate(n, row, width):
                recip_root(n, width)
                for k in range(KT):
                    for s in range(width // T):
                        cols = slice(s * T, (s + 1) * T)
                        dve.scalar_tensor_tensor(out=Y[:, k, cols], in0=Y[:, k, cols], scalar=AB[:, row, k, s:s + 1],
                                                 in1=RT[:, cols], op0=ALU.mult, op1=ALU.mult).then_inc(S(f"norm{n}_scaled"), 1)

            def plain_norm(n, w, dst, sem):
                recip_root(n, T)
                for k in range(KT):
                    dve.scalar_tensor_tensor(out=dst[:, k, 0:T], in0=X[:, k, 0:T], scalar=w[:, k:k + 1], in1=RT[:, 0:T],
                                             op0=ALU.mult, op1=ALU.mult).then_inc(sem, 1)

            def mod(l):
                dve.wait_ge(unit_done, base[f"mod{l}"] + 24)
                if l > 0:
                    dve.wait_ge(S("norm3_out"), KT)
                bm = W(f"b_mod{l}", 48)
                m = dve.tensor_tensor(MOD[:, :, :], B[5][:, 0:96].rearrange("p (a b) -> p a b", b=2),
                                      bm.unsqueeze(2).to_broadcast([P, 48, 2]), ALU.add)
                m.then_inc(S("mod_ready"), 1)
                dve.wait_ge(S("mod_ready"), l + 1)
                for i, (row, pre) in enumerate(((8, True), (16, False), (32, True), (40, False))):
                    w = W(f"n{i}_{l}", KT).unsqueeze(2).to_broadcast([P, KT, 2])
                    if pre:
                        ins = dve.scalar_tensor_tensor(out=AB[:, i, :, :], in0=MOD[:, row:row + KT, :], scalar=1.0, in1=w,
                                                       op0=ALU.add, op1=ALU.mult)
                    else:
                        ins = dve.tensor_tensor(AB[:, i, :, :], MOD[:, row:row + KT, :], w, ALU.mult)
                    step(ins)

            def attention(l):
                us = att_of[l]

                def maxima(u):
                    dve.wait_ge(S("att_s"), u + 1)
                    nk = len(ATT[u][5]) * P
                    dve.tensor_reduce(stat[:, u % 4:u % 4 + 1], B[u % 2][:, 0:nk], AX.X, ALU.max, negate=True)\
                       .then_inc(S("att_m"), 1)

                def normalise(u):
                    nk = len(ATT[u][5]) * P
                    dve.wait_ge(S("att_exp"), u + 1)
                    step(dve.reciprocal(stat[:, 8 + u % 4:9 + u % 4], stat[:, 4 + u % 4:5 + u % 4]))
                    dve.tensor_scalar(PR[:, u % 2, 0:nk], PR[:, u % 2, 0:nk], stat[:, 8 + u % 4:9 + u % 4], None, ALU.mult)\
                       .then_inc(S("att_p"), 1)

                def store(u):
                    dve.wait_ge(S("att_o"), u + 1)
                    lo = DH * (ATT[u][1] % 2)
                    dve.tensor_copy(ATT[u][6], B[6 + u % 2][lo:lo + DH, 0:P]).then_inc(S("att_oc"), 1)

                n = len(us)
                for i in range(n + 3):
                    if i < n:
                        maxima(us[i])
                    if 1 <= i <= n:
                        normalise(us[i - 1])
                    if i >= 3:
                        store(us[i - 3])

            def gqa_prep():
                step(dve.tensor_scalar(qw[:, :], W("q_norm", 1), float(DH) ** -0.5, None, ALU.mult))
                tmp = SC[:, 0:T]
                for i in range(6):
                    dve.wait_ge(S("gqa_rt"), i + 1)
                    step(dve.reciprocal(RT[:, :], RT[:, :]))
                    dve.scalar_tensor_tensor(out=proj0(i), in0=proj0(i), scalar=qw[:, 0:1] if i < 4 else W("k_norm", 1),
                                             in1=RT[:, :], op0=ALU.mult, op1=ALU.mult).then_inc(S("gqa_n"), 1)
                    lat = proj0(i)[:, 0:T]
                    dve.wait_ge(S("gqa_sw"), i + 1)
                    step(dve.tensor_tensor(tmp, B[5][:, 0:T], C("sin", T), ALU.mult))
                    step(dve.tensor_tensor(lat, lat, C("cos", T), ALU.mult))
                    dve.tensor_tensor(lat, lat, tmp, ALU.add).then_inc(S("gqa_rot"), 1)

            def hgrn(d):
                nl = len(LEVELS)
                if d == 0:
                    dve.wait_ge(lin_free, tile_base["proj0"] + 10 + 4)
                    dve.tensor_scalar(HQ, HQ, float(DK) ** -0.5, None, ALU.mult).then_inc(S("hg_q"), 1)
                else:
                    dve.wait_ge(S("hg_done"), d)
                dve.memset(SC[:, :], 0.0)
                dve.wait_ge(S("hg_ln"), d + 1)
                step(dve.scalar_tensor_tensor(out=HZ[d], in0=HZ[d], scalar=0.0, in1=HX[0], op0=ALU.min, op1=ALU.subtract))
                for h in range(B_HEADS):
                    o, g = (HB[:, h, :], HZ[d][:, h, :]) if d == 0 else (HB[:, h, ::-1], HZ[d][:, h, ::-1])
                    ins = dve.tensor_tensor_scan(o, C("reset", TC), g, 0.0, ALU.mult, ALU.add)
                step(ins)

                def halves(ap, m):
                    v = ap.rearrange("p h (n s m) -> p (h n) s m", s=2, m=m)
                    return v[:, :, 0, :], v[:, :, 1, :]

                def split(ap, m):
                    first, second = halves(ap, m)
                    return (second, first) if d == 0 else (first, second)

                def differences(i):
                    m = LEVELS[i]
                    if i >= 3:
                        dve.wait_ge(S("hg_mm"), (d * nl + i - 1) * B_HEADS)
                    bq, bk = split(HB, m)
                    xq, xk = split(HX[i % 2], m)
                    edge = bk[:, :, m - 1:m] if d == 0 else bk[:, :, 0:1]
                    n = B_HEADS * TC // (2 * m)
                    dve.tensor_tensor(xq, bq, edge.to_broadcast([P, n, m]), ALU.subtract)
                    dve.tensor_tensor(xk, edge.to_broadcast([P, n, m]), bk, ALU.subtract).then_inc(S("hg_d"), 1)

                def products(i):
                    m = LEVELS[i]
                    dve.wait_ge(S("hg_e"), d * (nl - 1) + i)
                    xq, xk = split(HX[i % 2], m)
                    dve.tensor_tensor(xq, xq, split(HQ, m)[0], ALU.mult)
                    dve.tensor_tensor(xk, xk, split(HK, m)[1], ALU.mult).then_inc(S("hg_x"), 1)

                def take(i):
                    for h in range(B_HEADS):
                        n = (d * nl + i) * B_HEADS + h
                        dve.wait_ge(S("hg_mm"), n + 1)
                        mask = lmask[:, (d * nl + i) * P:(d * nl + i + 1) * P].unsqueeze(1).to_broadcast([P, 4, P])
                        dve.copy_predicated(SCv[:, h, :].rearrange("p (c t) -> p c t", t=P), mask,
                                            B[h][:, :].rearrange("p (c t) -> p c t", t=P)).then_inc(S("hg_cp"), 1)

                dve.wait_ge(S("hg_k"), d + 1)
                for i in range(1, nl + 2):
                    if i < nl:
                        differences(i)
                    if 2 <= i <= nl:
                        products(i - 1)
                    if i >= 2:
                        take(i - 2)
                take(nl - 1) if False else None
                dve.wait_ge(S("hg_e0"), d + 1)
                last = P - 1 if d == 0 else 0
                ends = HX[0].rearrange("p h (c t) -> p (h c) t", t=P)[:, :, last]
                step(dve.tensor_copy(DEC[:, :], ends))
                dve.tensor_tensor(HX[0], HX[0], HQ, ALU.mult)
                b = HB.rearrange("p h (c t) -> p (h c) t", t=P)
                dve.tensor_tensor(HX[1].rearrange("p h (c t) -> p (h c) t", t=P), b[:, :, last:last + 1].to_broadcast([P, 16, P]),
                                  b, ALU.subtract).then_inc(S("hg_dk"), 1)
                dve.wait_ge(S("hg_ek"), d + 1)
                dve.tensor_tensor(HX[1], HX[1], HK, ALU.mult).then_inc(S("hg_kt"), 1)
                for i in range(3):
                    for h in range(B_HEADS):
                        dve.wait_ge(S("hg_u"), d * 12 + i * B_HEADS + h + 1)
                        if i == 0:
                            ins = dve.tensor_copy(ST[:, h, :], B[h][:, 0:P])
                        else:
                            c = ORDER[d][i]
                            if h == 0:
                                dve.wait_ge(S("hg_s"), d * 12 + i * B_HEADS)
                            ins = dve.scalar_tensor_tensor(out=ST[:, h, :], in0=ST[:, h, :], scalar=DEC[:, 4 * h + c:4 * h + c + 1],
                                                           in1=B[h][:, 0:P], op0=ALU.mult, op1=ALU.add)
                        ins.then_inc(S("hg_s"), 1)

            def hgrn_norm():
                for h in range(B_HEADS):
                    dve.wait_ge(S("hg_rt"), h + 1)
                    step(dve.reciprocal(SCv[:, h, :], SCv[:, h, :]))
                    step(dve.scalar_tensor_tensor(out=MIX[:, 4 + h, :], in0=B[4 + h][:, :], scalar=W("out_norm", 1),
                                                  in1=SCv[:, h, :], op0=ALU.mult, op1=ALU.mult))
                    dve.tensor_tensor(MIX[:, 4 + h, :], MIX[:, 4 + h, :], HG[:, h, :], ALU.mult).then_inc(S("hg_mix"), 1)

            def conv_ffn(l, width):
                name = f"up{l}"
                t0 = tile_base[name]
                cw = W(f"conv{l}", 2 * FT * 4)
                seqs = width // T

                def pair(j, it):
                    dve.wait_ge(S("conv_c"), it * NSLOT + (l * FT + j + 1))
                    for w, dst, src in ((0, slice(1, T), slice(0, T - 1)), (2, slice(0, T - 1), slice(1, T))):
                        for t in range(2):
                            col = cw[:, bass.ds(it * (4 * NSLOT) + 4 * (t * FT + j) + w, 1)]
                            u = B[(t0 + 2 * j + t) % 4][:, 0:width].rearrange("p (s t) -> p s t", t=T)[:, :, src]
                            o = CONV[:, j % 2, t, 0:width].rearrange("p (s t) -> p s t", t=T)[:, :, dst]
                            ins = dve.scalar_tensor_tensor(out=o, in0=u, scalar=col, in1=o, op0=ALU.mult, op1=ALU.add)
                        if w == 0:
                            ins.then_inc(S("conv_l"), 1)
                            dve.wait_ge(S("conv_l"), it * NSLOT + (l * FT + j + 1))
                    ins.then_inc(S("conv_d"), 1)

                loops = FT // NSLOT
                with dve.Fori(0, loops) as it:
                    for j in range(NSLOT):
                        pair(j, it)
                for j in range(loops * NSLOT, FT):
                    pair(j, 0)

            def causal_conv(l):
                w = W(f"ml_conv{l}", 32)
                for i in range(8):
                    dve.wait_ge(S("ml_c"), 8 * l + i + 1)
                    u = B[(tile_base[f"tproj{l}"] + 4 + i) % 4]
                    for s in range(1, 4):
                        o = P2[:, 4 + i, s:T]
                        ins = dve.scalar_tensor_tensor(out=o, in0=u[:, 0:T - s], scalar=w[:, 4 * i + 3 - s:4 * i + 4 - s], in1=o,
                                                       op0=ALU.mult, op1=ALU.add)
                        if s < 3:
                            step(ins)
                    ins.then_inc(S("ml_cv"), 1)

            def gate_rows(l):
                dve.wait_ge(S("ml_ln"), l + 1)
                z, soft, bsum, a, m = (rows[0:12, 2, :], rows[0:12, 1, :], rows[0:12, 3, :], rows[0:4, 4, :], rows[0:4, 5, :])
                step(dve.tensor_scalar(z, B[5][0:12, T:TC], W(f"b_f{l}", 1)[0:12], 0.0, ALU.add, ALU.min))
                step(dve.tensor_tensor(z, z, soft, ALU.subtract))
                step(dve.tensor_tensor_scan(bsum, C("ones_row", T)[0:12], z, 0.0, ALU.mult, ALU.add))
                step(dve.tensor_tensor(a, rows[0:4, 0, :], bsum[0:4], ALU.subtract))
                step(dve.tensor_tensor_scan(m, a, a, 0.0, ALU.max, ALU.max))
                dve.tensor_tensor(rows[0:4, 2, :], bsum[0:4], m, ALU.add).then_inc(S("ml_bm"), 1)

            def mlstm(l):
                dve.wait_ge(S("ml_at"), l + 1)
                dve.tensor_copy(acol[:, :, :], B[4][:, 0:2 * ML_HEADS].rearrange("p (a b) -> p a b", a=2)).then_inc(S("ml_acol"), 1)
                dve.wait_ge(S("ml_acol"), l + 1)
                for h in range(ML_HEADS):
                    dve.wait_ge(S("ml_bc"), ML_HEADS * l + h + 1)
                    dve.tensor_copy(MH[:, h, :], B[4 + h][:, T:TC])
                    dve.tensor_scalar(MW[:, h, 0:T], B[4 + h][:, 0:T], acol[:, 0, h:h + 1], 0.0, ALU.add, ALU.min)
                    dve.tensor_scalar(MW[:, h, T:T + P], B[4 + h][:, P:T], acol[:, 1, h:h + 1], 0.0, ALU.add, ALU.min)\
                       .then_inc(S("ml_w"), 1)
                for h in range(ML_HEADS):
                    dve.wait_ge(S("ml_e"), ML_HEADS * l + h + 1)
                    dve.tensor_tensor(MW[:, h, 0:P], MW[:, h, 0:P], C("causal_mul", P), ALU.mult)
                    step(dve.tensor_tensor(MW[:, h, T:T + P], MW[:, h, T:T + P], C("causal_mul", P), ALU.mult))
                    dve.wait_ge(S("ml_s"), ML_HEADS * l + h + 1)
                    dve.scalar_tensor_tensor(out=MP[:, h, :], in0=B[h][:, 0:T + P], scalar=float(DK) ** -0.5, in1=MW[:, h, :],
                                             op0=ALU.mult, op1=ALU.mult).then_inc(S("ml_p"), 1)
                for h in range(ML_HEADS):
                    dve.wait_ge(S("ml_nd"), ML_HEADS * l + h + 1)
                    step(dve.scalar_tensor_tensor(out=MH[:, h, :], in0=B[h][:, T:TC], scalar=-1.0, in1=MH[:, h, :],
                                                  op0=ALU.mult, op1=ALU.min))
                    step(dve.tensor_tensor(MW[:, h, 0:T], B[h][:, T:TC], MH[:, h, :], ALU.min))
                    step(dve.reciprocal(MW[:, h, 0:T], MW[:, h, 0:T]))
                    dve.scalar_tensor_tensor(out=MH[:, h, :], in0=B[h][:, 0:T], scalar=-1.0, in1=MW[:, h, 0:T],
                                             op0=ALU.mult, op1=ALU.mult).then_inc(S("ml_h"), 1)
                for h in range(ML_HEADS):
                    dve.wait_ge(S("ml_rt"), ML_HEADS * l + h + 1)
                    step(dve.reciprocal(MP[:, h, 0:T], MP[:, h, 0:T]))
                    step(dve.scalar_tensor_tensor(out=MH[:, h, :], in0=MH[:, h, :], scalar=W(f"ml_g{l}", 4)[:, h:h + 1],
                                                  in1=MP[:, h, 0:T], op0=ALU.mult, op1=ALU.mult))
                    dve.tensor_tensor(mix_ml(h), MH[:, h, :], P2[:, 12 + h, :], ALU.mult).then_inc(S("ml_mix"), 1)

            def branch(l):
                t0 = tile_base[f"branch{l}"]
                for j in range(KT):
                    dve.wait_ge(unit_done, base[f"branch{l}"] + j + 1)
                    dst = (H[:, j, T:TC], PSC[:, 2 * (j % 2), :], PSC[:, 2 * (j % 2) + 1, :])
                    for b in range(3):
                        dve.tensor_tensor(dst[b], B[(t0 + 3 * j + b) % 4][:, 0:T], G2[:, 8 * b + j, :], ALU.mult).then_inc(lin_free, 1)
                    dve.wait_ge(lin_free, t0 + 3 * j + 3 + 4)
                    step(dve.tensor_tensor(dst[0], dst[0], dst[1], ALU.add))
                    dve.tensor_tensor(dst[0], dst[0], dst[2], ALU.add).then_inc(S("merged"), 1)

            def add_out(name, t0, k, bank, wait):
                dve.wait_ge(unit_done, wait)
                dve.tensor_tensor(X[:, k, 0:T], X[:, k, 0:T], B[bank][:, 0:T], ALU.add).then_inc(lin_free, 1)

            def add_down(u0, e=None):
                eu = 0 if e is None else e * PER_E
                with dve.Fori(0, 16 // NSLOT) as it:
                    for j in range(NSLOT // 2):
                        dve.wait_ge(unit_done, it * NSLOT + (u0 + 2 * j + 2) + eu)
                        x = X[:, bass.ds(it * (NSLOT // 2) + j, 1), 0:T].rearrange("p a t -> p (a t)")
                        dve.tensor_tensor(x, x, B[j % 2][:, 0:T], ALU.add).then_inc(lin_free, 1)

            def swiglu(name, sw0, width, e=None):
                t0 = tile_base[name]
                n = FT if e is None else ET
                es = 0 if e is None else e * ET

                def pair(j, it):
                    dve.wait_ge(S("sw_s"), it * NSLOT + (sw0 + j + 1) + es)
                    g = CONV[:, j % 2, 0, 0:width]
                    if e is not None and width == T:
                        dve.tensor_tensor(g, g, GW[:, :], ALU.mult).then_inc(S("moe_g"), 1)
                        dve.wait_ge(S("moe_g"), it * NSLOT + (j + 1) + es)
                    dve.tensor_tensor(PROJ[:, bass.ds(it * (NSLOT * width) + j * width, width)], g,
                                      B[(t0 + 2 * j + 1) % 4][:, 0:width], ALU.mult)\
                       .then_inc(lin_free, 2)

                loops = n // NSLOT
                with dve.Fori(0, loops) as it:
                    for j in range(NSLOT):
                        pair(j, it)
                for j in range(loops * NSLOT, n):
                    pair(j, 0)

            def router():
                dve.wait_ge(S("rt_mm"), 1)
                for j in range(2):
                    r = rt[:, j, :]
                    step(dve.tensor_tensor(r[:, 0:8], B[5][:, 8 * j:8 * j + 8], W("b_router", 8), ALU.add))
                    step(dve.max(r[:, 8:16], r[:, 0:8]))
                    step(dve.max_index(widx[:, j, :], r[:, 8:16], r[:, 0:8]))
                    step(dve.tensor_copy(r[:, 16:18], widx[:, j, 0:2]))
                    dve.tensor_tensor(r[:, 18:19], r[:, 9:10], r[:, 8:9], ALU.subtract).then_inc(S("rt_d"), 1)
                for j in range(2):
                    r = rt[:, j, :]
                    dve.wait_ge(S("rt_e"), j + 1)
                    step(dve.tensor_scalar(r[:, 22:23], r[:, 19:20], 1.0, None, ALU.add))
                    step(dve.reciprocal(r[:, 20:21], r[:, 22:23]))
                    step(dve.tensor_tensor(r[:, 21:22], r[:, 20:21], r[:, 19:20], ALU.mult))
                    for i in range(2):
                        step(dve.tensor_scalar(r[:, 32 + 8 * i:40 + 8 * i], C("iota", 8), r[:, 16 + i:17 + i], r[:, 20 + i:21 + i],
                                               ALU.is_equal, ALU.mult))
                        step(dve.tensor_scalar(rsel[:, j, i, :], C("iota", 8), r[:, 16 + i:17 + i], None, ALU.is_equal))
                    step(dve.tensor_tensor(r[:, 24:32], rsel[:, j, 0, :], rsel[:, j, 1, :], ALU.add))
                    dve.tensor_tensor(r[:, 48:56], r[:, 32:40], r[:, 40:48], ALU.add).then_inc(S("rt_w"), 1)
                dve.wait_ge(S("rt_t"), 1)
                step(dve.tensor_copy(wrow[:, :], B[6][0:N_EXPERTS, 0:T]))
                dve.tensor_tensor(WD.rearrange("p (e t) -> p e t", t=T), wrow[:, :].unsqueeze(1).to_broadcast([N_EXPERTS, N_EXPERTS, T]),
                                  ident[0:N_EXPERTS, 0:N_EXPERTS].unsqueeze(2).to_broadcast([N_EXPERTS, N_EXPERTS, T]),
                                  ALU.mult).then_inc(S("rt_wr"), 1)

            dve.wait_ge(S("consts_in"), 16)
            dve.wait_ge(S("params_in"), 16)
            dve.wait_ge(S("masks_in"), 16)
            step(dve.tensor_copy(lmask[:, :], SC[:, :]))
            mod(0)
            modulate(0, 0, TC)
            gqa_prep()
            attention(0)
            hgrn(0)
            hgrn(1)
            hgrn_norm()
            gate(1, 1, TC)
            modulate(2, 2, TC)
            conv_ffn(0, TC)
            gate(3, 3, TC)
            mod(1)
            modulate(4, 0, TC)
            attention(1)
            gate(5, 1, T)
            modulate(6, 2, T)
            conv_ffn(1, T)
            gate(7, 3, T)
            for l in range(DEPTH):
                plain_norm(8 + 2 * l, W(f"mix_g{l}", KT), H, S(f"norm{8 + 2 * l}_out"))
                gate_rows(l)
                causal_conv(l)
                mlstm(l)
                attention(2 + l)
                branch(l)
                name = f"twout{l}"
                for k in range(KT):
                    add_out(name, tile_base[name], k, (tile_base[name] + k) % 4, base[name] + k // 2 + 1)
                plain_norm(9 + 2 * l, W(f"ffn_g{l}", KT), H, S(f"norm{9 + 2 * l}_out"))
                if l == 0:
                    swiglu("swup", 0, T)
                    add_down(base["swdown"])
            router()
            dve.wait_ge(S("mo_n"), 1)
            for j in range(2):
                step(dve.tensor_tensor(rt[:, j, 8:16], B[5][:, 32 + 8 * j:40 + 8 * j], rt[:, j, 24:32], ALU.mult))
                step(dve.tensor_scalar(rt[:, j, 56:64], rt[:, j, 8:16], -1.0, None, ALU.add))
            dve.tensor_scalar(many[:, :], B[5][:, 48:56], float(CAP), None, ALU.is_gt).then_inc(S("mo_many"), 1)
            dve.wait_ge(S("mo_many"), 1)
            dve.sem_inc(S("mo_sc"), 4)
            with dve.Fori(0, N_EXPERTS) as e:
                dve.wait_ge(S("mo_sc"), e * 4 + 4)
                for j in range(2):
                    slot, weight = rt[:, j, bass.ds(e + 56, 1)], rt[:, j, bass.ds(e + 48, 1)]
                    dve.tensor_scalar(SEL[:, j, :], C("iota", CAP), slot, None, ALU.is_equal)
                    ins = dve.tensor_scalar(SELW[:, j, :], C("iota", CAP), slot, weight, ALU.is_equal, ALU.mult)
                ins.then_inc(S("mo_sel"), 1)
                dve.wait_ge(S("mo_a"), e + 1)
                dve.tensor_copy(GW[:, :], B[5][:, T:TC])
                dve.tensor_copy(SELT, B[5][0:CAP, 0:T]).then_inc(S("mo_selt"), 1)
                dve.wait_ge(S("mo_selt"), e + 1)
                dense = dve.value_load(many[0:1, bass.ds(e, 1)], min_val=0, max_val=1)
                with dve.If(dense):
                    swiglu("moe_up", FT, T, e)
                    add_down(MOE0 + ET, e)
                    dve.sem_inc(S("mo_sc"), 4)
                with dve.Else():
                    swiglu("moe_up", FT, CAP, e)
                    dve.sem_inc(S("moe_g"), ET)
                    for i in range(4):
                        dve.wait_ge(S("mo_s"), e * 4 + i + 1)
                        x = X[:, 2 * i:2 * i + 2, 0:T]
                        dve.tensor_tensor(x, x, B[6 + i % 2][:, :].rearrange("p (k t) -> p k t", t=T), ALU.add).then_inc(S("mo_sc"), 1)
            plain_norm(12, W("final_g", KT), Y, S("out_ready"))

        @block.gpsimd
        def _(pool):
            step = Chain(pool, "pool_step")

            def residual(n, width):
                for k in range(KT):
                    pool.wait_ge(S(f"norm{n}_scaled"), (k + 1) * (width // T))
                    pool.tensor_tensor(X[:, k, 0:width], X[:, k, 0:width], Y[:, k, 0:width], ALU.add).then_inc(S(f"norm{n}_out"), 1)

            def conv_ffn(l, width):
                t0 = tile_base[f"up{l}"]

                def pair(j, it):
                    pool.wait_ge(lin_free, it * (2 * NSLOT) + (t0 + 2 * j + 2 + 4))
                    pool.tensor_tensor(PROJ[:, bass.ds(it * (NSLOT * width) + j * width, width)], CONV[:, j % 2, 0, 0:width],
                                       CONV[:, j % 2, 1, 0:width], ALU.mult).then_inc(S("ffn_hid"), 1)

                loops = FT // NSLOT
                with pool.Fori(0, loops) as it:
                    for j in range(NSLOT):
                        pair(j, it)
                for j in range(loops * NSLOT, FT):
                    pair(j, 0)

            def window_means(l):
                pool.wait_ge(lin_free, tile_base[f"tproj{l}"] + 4 + 4)
                for g, w in enumerate(POOL_WINDOWS):
                    src, s, n = P2[:, g, :], 1, 0
                    while s < w:
                        dst = PSC[:, n % 2, :]
                        pool.tensor_copy(dst[:, 0:s], src[:, 0:s])
                        step(pool.tensor_tensor(dst[:, s:T], src[:, s:T], src[:, 0:T - s], ALU.add))
                        src, s, n = dst, 2 * s, n + 1
                    step(pool.tensor_tensor(PSC[:, 2, :], src, C("rcount", 4 * T)[:, g * T:(g + 1) * T], ALU.mult))
                    step(pool.tensor_tensor(P2[:, g, :], PSC[:, 2, :], P2[:, g, :], ALU.subtract))
                    pool.sem_inc(S("pool_d"), 1)

            pool.sem_inc(S("ffn_hid"), 2)
            pool.dma_start(SC[:, :], dram["level_masks"]).then_inc(S("masks_in"), 16)
            for h in range(2):
                pool.dma_start(BIAS[:, h, :], dram["bias"][h]).then_inc(S(f"bias{h}_in"), 16)
            residual(1, TC)
            conv_ffn(0, TC)
            residual(3, TC)
            for h in range(2, C_HEADS):
                pool.wait_ge(S("att_s"), att_of[1][0] + 2 * (h - 1))
                pool.dma_start(BIAS[:, h % 2, :], dram["bias"][h]).then_inc(S(f"bias{h % 2}_in"), 16)
            residual(5, T)
            conv_ffn(1, T)
            residual(7, T)
            for l in range(DEPTH):
                window_means(l)
    return nc


def constants():
    c = np.zeros((P, CONSTS["_end"]), np.float32)

    def put(name, a):
        c[0:a.shape[0], CONSTS[name]:CONSTS[name] + a.shape[1]] = a

    i = np.arange(P)
    put("ident", np.eye(P))
    put("mean_d", np.full((P, P), 1 / D))
    put("mean_dk", np.full((P, P), 1 / DK))
    put("mean_dh", (i[:, None] // DH == i[None, :] // DH) / DH)
    put("ones", np.ones((P, P)))
    half = DH // 2
    swap = np.zeros((P, P))
    for t in range(P):
        swap[t + half if t % DH < half else t - half, t] = -1.0 if t % DH < half else 1.0
    put("swap", swap)
    t = np.arange(T)
    n_freq = DH // 4
    freq = np.float32(10000.0) ** (-np.arange(n_freq, dtype=np.float32) / np.float32(n_freq))
    ang = np.concatenate([(t // GRID_W)[None, :].astype(np.float32) * freq[:, None],
                          (t % GRID_W)[None, :].astype(np.float32) * freq[:, None]]).astype(np.float32)
    put("cos", np.cos(ang)[i % half])
    put("sin", np.sin(ang)[i % half])
    put("reset", np.broadcast_to((np.arange(TC) % P != 0).astype(np.float32), (P, TC)))
    put("causal_add", np.where(i[None, :] <= i[:, None], 0.0, NEG))
    put("causal_mul", (i[:, None] <= i[None, :]).astype(np.float32))
    put("nsel", -np.eye(12))
    put("rcount", np.broadcast_to(np.concatenate([1.0 / np.minimum(t + 1, w) for w in POOL_WINDOWS])[None, :], (P, 4 * T)))
    put("ones_row", np.ones((P, T)))
    put("iota", np.broadcast_to(np.arange(CAP)[None, :], (P, CAP)))
    put("eps", np.full((P, 1), EPS))
    m = np.zeros((P, 2, len(LEVELS), P), np.float32)
    for n, b in enumerate(LEVELS):
        if b == 0:
            m[:, :, n, :] = np.eye(P)[:, None, :]
        else:
            same = i[:, None] // (2 * b) == i[None, :] // (2 * b)
            first = (i // b) % 2 == 0
            m[:, 0, n, :] = same & first[:, None] & ~first[None, :]
            m[:, 1, n, :] = same & ~first[:, None] & first[None, :]
    return c, m.reshape(P, -1)


def layout(x):
    f = {k: np.asarray(v) for k, v in x.items()}
    out = {}

    def tiles(w, n=2 * P):
        k, cols = w.shape
        return np.ascontiguousarray(w.reshape(k // P, P, cols // n, n).transpose(2, 1, 0, 3)).reshape(cols // n, P, -1)

    def paired(a, b):
        k, cols = a.shape
        r = np.empty((cols // P, P, k // P, 2, P), np.float32)
        for s, w in enumerate((a, b)):
            r[:, :, :, s, :] = w.reshape(k // P, P, cols // P, P).transpose(2, 1, 0, 3)
        return r.reshape(cols // P, P, -1)

    def down(w):
        k, cols = w.shape
        h = k // P // 2
        return np.ascontiguousarray(w.reshape(2, h, P, cols // P, P).transpose(3, 0, 2, 1, 4)).reshape(2 * cols // P, P, h * P)

    w = f["even_w_in"][0]
    aq, ak, av, bq, bf, bb, bi, bg = (w[:, a:b] for a, b in ((0, 512), (512, 640), (640, 768), (768, 1280), (1280, 1792),
                                                            (1792, 2304), (2304, 2816), (2816, 3328)))
    kk = [ak[:, 0:DH], ak[:, 0:DH], ak[:, DH:], ak[:, DH:]]
    out["proj0"] = tiles(np.concatenate([aq, *kk, bq, bf, bb, bg, bi, av, av], axis=1))
    out["proj1"] = tiles(f["odd_w_qkv"][0])
    out["wout0"], out["wout1"] = tiles(f["even_w_out"][0]), tiles(f["odd_w_out"][0])
    for l in range(DEPTH):
        out[f"mod{l}"] = tiles(f["w_mod"][l])
        out[f"up{l}"] = paired(f["ffn_w_up"][l][:, :D_FF], f["ffn_w_up"][l][:, D_FF:])
        out[f"down{l}"] = down(f["ffn_w_down"][l])
        w = f["w_in_2"][l]
        o = np.cumsum([0, 512, 512, 512, 512, 512, 4, 4, 512, 512, 512, 8, 3 * D])
        part = [w[:, o[i]:o[i + 1]] for i in range(12)]
        up, mq, mk, mv, mo, mi, mf, fq, fk, fv, ff, gates = part
        out[f"tproj{l}"] = tiles(np.concatenate([up, mq, mk, mo, fq, fk, mv, fv], axis=1))
        out[f"gates{l}"] = tiles(gates)
        b = np.stack([f[f"w_br_{n}_2"][l] for n in ("pool", "ml", "fox")])
        out[f"branch{l}"] = np.ascontiguousarray(b.reshape(3, 4, P, KT, P).transpose(3, 2, 0, 1, 4)).reshape(KT, P, 12 * P)
        out[f"twout{l}"] = tiles(f["w_out_2"][l])
    out["swup"] = paired(f["ff_w_gate_2"][0], f["ff_w_up_2"][0])
    out["swdown"] = down(f["ff_w_down_2"][0])
    out["moe_up"] = np.concatenate([paired(f["moe_w_gate_2"][0][e], f["moe_w_up_2"][0][e]) for e in range(N_EXPERTS)])
    out["moe_down"] = np.concatenate([down(f["moe_w_down_2"][0][e]) for e in range(N_EXPERTS)])

    tok = np.concatenate([f["x"][0], f["ctx"][0]])
    out["xT"] = np.ascontiguousarray(tok.reshape(TC, KT, P).transpose(2, 1, 0)).reshape(P, -1)

    p = np.zeros((P, PARAMS["_end"]), np.float32)

    def put(name, a):
        p[0:a.shape[0], PARAMS[name]:PARAMS[name] + a.shape[1]] = a

    def cols(v):
        return v.reshape(-1, P).T

    put("c", np.stack([cols(f["c"][0]), cols(f["c_ctx"])], axis=2).reshape(P, -1))
    for l in range(DEPTH):
        put(f"b_mod{l}", cols(f["b_mod"][l]))
        for i, n in enumerate(("norm_pre_mix", "norm_post_mix", "norm_pre_ffn", "norm_post_ffn")):
            put(f"n{i}_{l}", cols(f[n][l]))
        taps = np.concatenate([f["ffn_conv_w"][l], f["ffn_conv_b"][l][None]])
        put(f"conv{l}", taps.reshape(4, 2 * FT, P).transpose(2, 1, 0).reshape(P, -1))
        put(f"mix_g{l}", cols(f["mix_norm_g_2"][l]))
        put(f"ffn_g{l}", cols(f["ffn_norm_g_2"][l]))
        put(f"pool_scale{l}", cols(f["pool_scale_2"][l]))
        put(f"ml_conv{l}", f["ml_conv_w_2"][l].reshape(4, 8, P).transpose(2, 1, 0).reshape(P, -1))
        put(f"ml_g{l}", cols(f["ml_norm_g_2"][l]))
        put(f"b_i{l}", f["ml_b_i_2"][l][:, None])
        put(f"b_f{l}", np.concatenate([f["ml_b_f_2"][l], f["fox_b_f_2"][l]])[:, None])
        w = f["w_in_2"][l]
        small = np.concatenate([w[:, 2560:2564], w[:, 2564:2568], w[:, 4104:4112]], axis=1)
        put(f"w_small{l}", small.reshape(KT, P, 16).transpose(1, 0, 2).reshape(P, -1))
        put(f"w_grp{l}", f["pool_w_grp_2"][l].transpose(1, 0, 2).reshape(P, -1))
    put("q_norm", np.tile(f["even_q_norm"][0], 2)[:, None])
    put("k_norm", np.tile(f["even_k_norm"][0], 2)[:, None])
    put("out_norm", f["hgrn_out_norm"][0][:, None])
    put("w_router", f["moe_w_router_2"][0].reshape(KT, P, N_EXPERTS).transpose(1, 0, 2).reshape(P, -1))
    put("b_router", np.broadcast_to(f["moe_b_router_2"][0], (P, N_EXPERTS)))
    put("final_g", cols(f["final_norm_g_2"]))
    out["params"] = p
    out["consts"], out["level_masks"] = constants()

    t = np.arange(T)
    r, c = t // GRID_W, t % GRID_W
    start = np.clip(c - NA_COLS // 2, 0, GRID_W - NA_COLS)
    dy = r[None, :] - r[:, None] + NA_ROWS - 1
    dx = c[None, :] - c[:, None] + NA_COLS - 1
    inside = (c[None, :] >= start[:, None]) & (c[None, :] < start[:, None] + NA_COLS)
    bias = np.full((C_HEADS, T, T), NEG, np.float32)
    bias[:, inside] = f["odd_rpb"][0][:, dy[inside], dx[inside]]
    out["bias"] = np.ascontiguousarray(bias.reshape(C_HEADS, 2, P, T).transpose(0, 2, 1, 3)).reshape(C_HEADS, P, 2 * T)
    return out


def kernel(**inputs):
    import concourse.bacc as bacc
    from concourse.bass_utils import run_bass_kernel_spmd

    arrays = layout(inputs)
    nc = bacc.Bacc("TRN2", target_bir_lowering=False, num_devices=1)
    dram = {n: nc.dram_tensor("in_" + n, a.shape, mybir.dt.from_np(a.dtype), kind="ExternalInput").ap() for n, a in arrays.items()}
    out = nc.dram_tensor("out_x", (P, KT, T), mybir.dt.float32, kind="ExternalOutput").ap()
    build(nc, dram, out)
    r = run_bass_kernel_spmd(nc, [{"in_" + n: a for n, a in arrays.items()}], core_ids=[0])
    y = r.results[0]["out_x"]
    return np.ascontiguousarray(y.transpose(2, 1, 0)).reshape(1, T, D)
```
